# Optimizing a Trainium2 kernel written in Bass

```python
import math
import jax, jax.numpy as jnp
from jax import lax
import numpy as np

D_MODEL = 1024
BATCH = 1
SEQ = 1024
DEPTH = 1

HEAD_DIM = 64
SWA_Q_HEADS = 8
SWA_KV_HEADS = 2
SWA_GROUP = SWA_Q_HEADS // SWA_KV_HEADS
WINDOW = 128
SWA_BLOCK = 128
DIFF_HEADS = 4
DIFF_QBLOCK = 128
ROPE_THETA = 10000.0
N_EXPERTS = 32
TOP_K = 4
D_FF = D_MODEL
SWIGLU_LIMIT = 7.0
SWIGLU_ALPHA = 1.702
MOE_BLOCK = 128
RMS_EPS = 1e-5

SWA_Q_W = SWA_Q_HEADS * HEAD_DIM
SWA_KV_W = SWA_KV_HEADS * HEAD_DIM
DIFF_QK_W = DIFF_HEADS * 2 * HEAD_DIM
DIFF_V_W = DIFF_HEADS * 2 * HEAD_DIM
IN_SPLITS = (SWA_Q_W, SWA_KV_W, SWA_KV_W, DIFF_QK_W, DIFF_QK_W, DIFF_V_W, D_MODEL, D_MODEL)
IN_WIDTH = sum(IN_SPLITS)

kernel_name = "hybrid_swa_sink_diffattn_gated_moe"

def rms_norm(x, g):
    xf = x.astype(jnp.float32)
    y = xf * lax.rsqrt(jnp.mean(xf * xf, axis=-1, keepdims=True) + RMS_EPS)
    return (y * g.astype(jnp.float32)).astype(x.dtype)

def rope_tables(seq, dim):
    pos = jnp.arange(seq, dtype=jnp.float32)
    inv_freq = ROPE_THETA ** (-jnp.arange(0, dim, 2, dtype=jnp.float32) / dim)
    ang = pos[:, None] * inv_freq[None, :]
    return jnp.cos(ang), jnp.sin(ang)

def apply_rope(x, cos, sin):
    x1, x2 = jnp.split(x.astype(jnp.float32), 2, axis=-1)
    c = cos[None, :, None, :]
    s = sin[None, :, None, :]
    return jnp.concatenate([x1 * c - x2 * s, x2 * c + x1 * s], axis=-1).astype(x.dtype)

def sliding_window_attention(q, k, v, sinks):
    B, S = q.shape[0], q.shape[1]
    nb = S // SWA_BLOCK
    qb = q.reshape(B, nb, SWA_BLOCK, SWA_KV_HEADS, SWA_GROUP, HEAD_DIM)
    kb = k.reshape(B, nb, SWA_BLOCK, SWA_KV_HEADS, HEAD_DIM)
    vb = v.reshape(B, nb, SWA_BLOCK, SWA_KV_HEADS, HEAD_DIM)

    def with_prev(t):
        prev = jnp.pad(t[:, :-1], ((0, 0), (1, 0), (0, 0), (0, 0), (0, 0)))
        return jnp.concatenate([prev, t], axis=2)

    kc, vc = with_prev(kb), with_prev(vb)
    s = jnp.einsum('bnqhgd,bnkhd->bnhgqk', qb, kc).astype(jnp.float32) * (HEAD_DIM ** -0.5)
    qi = jnp.arange(SWA_BLOCK)[:, None] + SWA_BLOCK
    kj = jnp.arange(2 * SWA_BLOCK)[None, :]
    band = (kj <= qi) & (qi - kj < WINDOW)
    has_prev = (jnp.arange(nb)[:, None, None] > 0) | (kj[None] >= SWA_BLOCK)
    mask = band[None] & has_prev
    s = jnp.where(mask[None, :, None, None], s, -jnp.inf)
    sink = sinks.astype(jnp.float32).reshape(SWA_KV_HEADS, SWA_GROUP)
    sink_b = jnp.broadcast_to(sink[None, None, :, :, None, None], s.shape[:-1] + (1,))
    p = jax.nn.softmax(jnp.concatenate([s, sink_b], axis=-1), axis=-1)[..., :-1]
    o = jnp.einsum('bnhgqk,bnkhd->bnqhgd', p.astype(v.dtype), vc)
    return o.reshape(B, S, SWA_Q_W)

def diff_attention(q, k, v, lam):
    B, S = q.shape[0], q.shape[1]
    nb = S // DIFF_QBLOCK
    kpos = jnp.arange(S)
    scale = HEAD_DIM ** -0.5

    def block(i):
        start = i * DIFF_QBLOCK
        qi = lax.dynamic_slice_in_dim(q, start, DIFF_QBLOCK, axis=1)
        s = jnp.einsum('bqhcd,bkhcd->bhcqk', qi, k).astype(jnp.float32) * scale
        qpos = start + jnp.arange(DIFF_QBLOCK)
        causal = kpos[None, :] <= qpos[:, None]
        p = jax.nn.softmax(jnp.where(causal, s, -jnp.inf), axis=-1)
        a = p[:, :, 0] - lam * p[:, :, 1]
        return jnp.einsum('bhqk,bkhe->bqhe', a.astype(v.dtype), v)

    o = lax.map(block, jnp.arange(nb))
    return o.transpose(1, 0, 2, 3, 4).reshape(B, S, DIFF_HEADS, 2 * HEAD_DIM)

def moe_ffn(x, router_w, router_b, w1, b1, w2, b2):
    B, S, D = x.shape
    N = B * S
    xf = x.reshape(N, D)
    logits = (xf @ router_w + router_b).astype(jnp.float32)
    top_vals, top_idx = lax.top_k(logits, TOP_K)
    gates = jax.nn.softmax(top_vals, axis=-1)
    A = N * TOP_K
    flat_e = top_idx.reshape(A).astype(jnp.int32)
    flat_tok = jnp.arange(A, dtype=jnp.int32) // TOP_K
    flat_w = gates.reshape(A)
    order = jnp.argsort(flat_e, stable=True)
    se, stok, sw = flat_e[order], flat_tok[order], flat_w[order]
    counts = jnp.bincount(flat_e, length=N_EXPERTS).astype(jnp.int32)
    padded = (counts + MOE_BLOCK - 1) // MOE_BLOCK * MOE_BLOCK
    grp_start = jnp.cumsum(counts) - counts
    pad_end = jnp.cumsum(padded)
    pad_start = pad_end - padded
    dest = pad_start[se] + jnp.arange(A, dtype=jnp.int32) - grp_start[se]
    n_rows = (-(-A // MOE_BLOCK) + N_EXPERTS) * MOE_BLOCK
    n_blocks = n_rows // MOE_BLOCK
    row_tok = jnp.zeros((n_rows,), jnp.int32).at[dest].set(stok)
    row_w = jnp.zeros((n_rows,), jnp.float32).at[dest].set(sw)
    block_start = jnp.arange(n_blocks, dtype=jnp.int32) * MOE_BLOCK
    block_e = jnp.minimum(jnp.searchsorted(pad_end, block_start, side='right'), N_EXPERTS - 1)
    xb = xf[row_tok].reshape(n_blocks, MOE_BLOCK, D)

    def expert_block(args):
        xblk, e = args
        h = xblk @ w1[e] + b1[e]
        g, u = jnp.split(h, 2, axis=-1)
        g = jnp.minimum(g, SWIGLU_LIMIT)
        u = jnp.clip(u, -SWIGLU_LIMIT, SWIGLU_LIMIT)
        act = g * jax.nn.sigmoid(SWIGLU_ALPHA * g) * (u + 1.0)
        return act @ w2[e] + b2[e]

    yb = lax.map(expert_block, (xb, block_e)).reshape(n_rows, D)
    y = jnp.zeros((N, D), yb.dtype).at[row_tok].add(yb * row_w[:, None].astype(yb.dtype))
    return y.reshape(B, S, D).astype(x.dtype)

def setup_inputs(seed: int = 0) -> dict:
    key = jax.random.key(seed)
    ks = jax.random.split(key, 22)
    n = lambda k, shape, s: jax.random.normal(k, shape, jnp.float32) * s
    L, D, E, F = DEPTH, D_MODEL, N_EXPERTS, D_FF
    return {
        "x": n(ks[0], (BATCH, SEQ, D), 1.0),
        "attn_norm_g": 1.0 + n(ks[1], (L, D), 0.01),
        "w_in": n(ks[2], (L, D, IN_WIDTH), D ** -0.5),
        "b_in": n(ks[3], (L, IN_WIDTH), 0.02),
        "swa_sinks": n(ks[4], (L, SWA_Q_HEADS), 0.5),
        "diff_lambda_q1": n(ks[5], (L, HEAD_DIM), 0.1),
        "diff_lambda_k1": n(ks[6], (L, HEAD_DIM), 0.1),
        "diff_lambda_q2": n(ks[7], (L, HEAD_DIM), 0.1),
        "diff_lambda_k2": n(ks[8], (L, HEAD_DIM), 0.1),
        "diff_subln_g": 1.0 + n(ks[9], (L, 2 * HEAD_DIM), 0.01),
        "w_swa_out": n(ks[10], (L, SWA_Q_W, D), SWA_Q_W ** -0.5),
        "w_diff_out": n(ks[11], (L, DIFF_V_W, D), DIFF_V_W ** -0.5),
        "w_o": n(ks[12], (L, D, D), D ** -0.5),
        "ffn_norm_g": 1.0 + n(ks[13], (L, D), 0.01),
        "router_w": n(ks[14], (L, D, E), D ** -0.5),
        "router_b": n(ks[15], (L, E), 0.01),
        "w1": n(ks[16], (L, E, D, 2 * F), D ** -0.5),
        "b1": n(ks[17], (L, E, 2 * F), 0.01),
        "w2": n(ks[18], (L, E, F, D), F ** -0.5),
        "b2": n(ks[19], (L, E, D), 0.01),
        "final_norm_g": 1.0 + n(ks[20], (D,), 0.01),
    }

def reference(x, attn_norm_g, w_in, b_in, swa_sinks, diff_lambda_q1, diff_lambda_k1,
              diff_lambda_q2, diff_lambda_k2, diff_subln_g, w_swa_out, w_diff_out, w_o,
              ffn_norm_g, router_w, router_b, w1, b1, w2, b2, final_norm_g):
    B, S = x.shape[0], x.shape[1]
    cos, sin = rope_tables(S, HEAD_DIM)
    split_at = [int(i) for i in np.cumsum(IN_SPLITS)[:-1]]
    f32 = jnp.float32
    for l in range(DEPTH):
        h = rms_norm(x, attn_norm_g[l])
        proj = h @ w_in[l] + b_in[l]
        qa, ka, va, qb, kb, vb, ga, gb = jnp.split(proj, split_at, axis=-1)
        qa = apply_rope(qa.reshape(B, S, SWA_Q_HEADS, HEAD_DIM), cos, sin)
        ka = apply_rope(ka.reshape(B, S, SWA_KV_HEADS, HEAD_DIM), cos, sin)
        va = va.reshape(B, S, SWA_KV_HEADS, HEAD_DIM)
        ya = sliding_window_attention(qa, ka, va, swa_sinks[l]) @ w_swa_out[l]
        qb = apply_rope(qb.reshape(B, S, 2 * DIFF_HEADS, HEAD_DIM), cos, sin).reshape(B, S, DIFF_HEADS, 2, HEAD_DIM)
        kb = apply_rope(kb.reshape(B, S, 2 * DIFF_HEADS, HEAD_DIM), cos, sin).reshape(B, S, DIFF_HEADS, 2, HEAD_DIM)
        vb = vb.reshape(B, S, DIFF_HEADS, 2 * HEAD_DIM)
        lam_init = 0.8 - 0.6 * math.exp(-0.3 * l)
        lam = (jnp.exp(jnp.sum(diff_lambda_q1[l].astype(f32) * diff_lambda_k1[l].astype(f32)))
               - jnp.exp(jnp.sum(diff_lambda_q2[l].astype(f32) * diff_lambda_k2[l].astype(f32)))
               + lam_init)
        ob = rms_norm(diff_attention(qb, kb, vb, lam), diff_subln_g[l]) * (1.0 - lam_init)
        yb = ob.reshape(B, S, DIFF_V_W) @ w_diff_out[l]
        mixed = jax.nn.sigmoid(ga) * ya + jax.nn.sigmoid(gb) * yb
        x = x + mixed @ w_o[l]
        x = x + moe_ffn(rms_norm(x, ffn_norm_g[l]), router_w[l], router_b[l], w1[l], b1[l], w2[l], b2[l])
    return rms_norm(x, final_norm_g)


_drawn_inputs = setup_inputs


def setup_inputs(seed=0):
    import zlib

    import numpy as np

    out = dict(_drawn_inputs(seed))
    spreads = {}
    factors = {'swa_sinks': 7.391,
     'diff_lambda_q1': 29.08,
     'diff_subln_g': 7.894,
     'b1': 8.0,
     'b2': 46.537,
     'final_norm_g': 200.0,
     'ffn_norm_g': 2.922,
     'router_b': 8.872}
    for name, (base, spread) in spreads.items():
        noise = np.random.default_rng([zlib.crc32(name.encode()), seed]).standard_normal(out[name].shape)
        drawn = base * np.exp(spread * noise) if base else spread * noise
        out[name] = __import__('jax').numpy.asarray(drawn.astype(out[name].dtype))
    for name, factor in factors.items():
        out[name] = (out[name] * factor).astype(out[name].dtype)
    return out
```

```python
import numpy as np
from contextlib import ExitStack

import concourse.bass as bass
from concourse import mybir

F32 = mybir.dt.float32
BF16 = mybir.dt.bfloat16
I32 = mybir.dt.int32
U32 = mybir.dt.uint32
ALU = mybir.AluOpType
ACT = mybir.ActivationFunctionType
AX = mybir.AxisListType

P = 128
D = 1024
S = 1024
NT = S // P
KD = D // P
HD = 64
SWA_HEADS, SWA_KV = 8, 2
DIFF_HEADS = 4
NEXP, TOPK = 32, 4
FF = 1024
EPS = 1e-5
ATT_SCALE = HD ** -0.5
LAM_INIT = 0.8 - 0.6
NEG = -1.0e30
C_QA, C_KA, C_VA, C_QB, C_KB, C_VB, C_GA, C_GB, C_END = 0, 512, 640, 768, 1280, 1792, 2304, 3328, 4352
NCAT = C_GA
CHUNKS = [(C_QA, 512), (C_KA, 256), (C_QB, 512), (C_KB, 512), (C_VB, 512)]
TURNED_CHUNKS = 4
UNITS = [(kind, i, j) for i in range(NT) for j in range(4) for kind in ("swa", "diff")]
NU = len(UNITS)


def shape_constants():
    q, k = np.arange(P)[:, None], np.arange(P)[None, :]
    ident = np.eye(P, dtype=np.float32)
    causal = np.where(k <= q, 0.0, NEG).astype(np.float32)
    before = np.where(k > q, 0.0, NEG).astype(np.float32)
    pos = np.arange(S, dtype=np.float32)
    inv = np.float32(10000.0) ** (-np.arange(0, HD, 2, dtype=np.float32) / np.float32(HD))
    ang = (pos[:, None] * inv[None, :].astype(np.float32)).astype(np.float32)
    c, s = np.cos(ang).astype(np.float32), np.sin(ang).astype(np.float32)
    cos = np.concatenate([c, c], 1).reshape(NT, P, HD).transpose(1, 0, 2).reshape(P, NT * HD)
    sin = np.concatenate([-s, s], 1).reshape(NT, P, HD).transpose(1, 0, 2).reshape(P, NT * HD)
    return np.ascontiguousarray(np.concatenate([ident, causal, before], 1)), np.ascontiguousarray(np.concatenate([cos, sin], 1))


def units_before(kind, u):
    return sum(1 for x in UNITS[:u] if x[0] == kind)


def keys_of(unit):
    kind, i, _ = unit
    if kind == "diff":
        return list(range(i + 1))
    return [i - 1, i] if i else [0]


def program(nc, a, debug=None):
    with ExitStack() as kept:
        tabs_s = kept.enter_context(nc.sbuf_tensor("tabs_s", [P, 3 * P], F32))
        reg_h = kept.enter_context(nc.sbuf_tensor("reg_h", [P, 8192], F32))
        attention_half(nc, a, tabs_s, reg_h, debug)
        if debug != "x2":
            expert_half(nc, a, tabs_s, reg_h, debug)


def attention_half(nc, a, tabs_s, reg_h, debug=None):
    tabs, rope = shape_constants()
    tabs_d = nc.inline_tensor(tabs, name="masks_table").ap()
    rope_d = nc.inline_tensor(rope, name="rope_table").ap()
    ctx = ExitStack()
    with ctx:
        def sb(name, shape, dt=F32):
            return ctx.enter_context(nc.sbuf_tensor(name, shape, dt))

        def sem(name):
            return ctx.enter_context(nc.semaphore(name))

        bank = [ctx.enter_context(nc.psum_tensor(f"bank{i}", [P, 512], F32)) for i in range(8)]

        ident, causal, before = (tabs_s[:, i * P:(i + 1) * P] for i in range(3))
        small = sb("small", [P, 256])
        eps_c = small[:, 0:1]
        ss1, rms1, rstd1 = small[:, 8:16], small[:, 16:24], small[:, 24:32]
        lam_s, lam_e, neg_lam = small[:, 32:34], small[:, 34:36], small[:, 36:37]
        mx, nm, lsum, rinv = small[:, 40:44], small[:, 44:48], small[:, 48:52], small[:, 52:60]
        sink_e, coef = small[:, 60:64], small[:, 64:66]
        ssb, rmsb, rstdb = small[:, 72:104], small[:, 104:136], small[:, 136:168]
        sinks, neg_sinks = small[:, 168:176], small[:, 176:184]
        gate_bias = small[:, 184:200]
        lamv = sb("lamv", [P, 4 * HD])
        subln = sb("subln", [P, 2 * HD])
        early = sb("early", [P, D + NCAT + 2 * NT * HD])
        g1_b = early[:, 0:D]
        bias_b = early[:, D:D + NCAT]
        cos_s = early[:, D + NCAT:D + NCAT + NT * HD].rearrange("p (t d) -> p t d", t=NT)
        sin_s = early[:, D + NCAT + NT * HD:].rearrange("p (t d) -> p t d", t=NT)
        reg_qa = sb("reg_qa", [P, 4096])
        reg_qb = sb("reg_qb", [P, 4096])
        reg_ka = sb("reg_ka", [P, 2048])
        reg_kv = sb("reg_kv", [P, 8192])
        reg_w = sb("reg_w", [P, 8192])
        reg_p = sb("reg_p", [P, 8192])
        reg_g = sb("reg_g", [P, 2048])
        hT = reg_h[:, :].rearrange("p (k n) -> p k n", k=KD)
        x2 = reg_h[:, :].rearrange("p (t n) -> p t n", t=NT)
        qaT = reg_qa[:, :].rearrange("p (j n) -> p j n", j=4)
        qbT = reg_qb[:, :].rearrange("p (j n) -> p j n", j=4)
        kaT = reg_ka[:, 0:1024]
        va = reg_ka[:, 1024:2048].rearrange("p (t e) -> p t e", t=NT)
        kbT = reg_kv[:, 0:4096].rearrange("p (j n) -> p j n", j=4)
        vb = reg_kv[:, 4096:8192].rearrange("p (t e) -> p t e", t=NT)
        wo_s = reg_kv[:, :].rearrange("p (k n) -> p k n", k=KD)
        wch = [reg_w[:, i * 4096:(i + 1) * 4096] for i in range(2)]
        oan = reg_w[:, 0:4096].rearrange("p (t j e) -> p t j e", t=NT, j=4)
        obn = reg_w[:, 4096:8192].rearrange("p (t j e) -> p t j e", t=NT, j=4)
        mixT = reg_w[:, :].rearrange("p (k n) -> p k n", k=KD)
        xin = [reg_p[:, i * 1024:(i + 1) * 1024] for i in range(2)]
        hn = [reg_p[:, 2048 + i * 1024:2048 + (i + 1) * 1024] for i in range(2)]
        junk = reg_p[:, 4096:5120]
        biased = [reg_p[:, 5120 + i * 512:5120 + (i + 1) * 512] for i in range(2)]
        roped = [reg_p[:, 6144 + i * 512:6144 + (i + 1) * 512] for i in range(2)]
        rot = [reg_p[:, 7168 + i * 512:7168 + (i + 1) * 512] for i in range(2)]
        probs = [[reg_p[:, (2 * b + c) * 1024:(2 * b + c + 1) * 1024] for c in range(2)] for b in range(2)]
        pT = [reg_p[:, 4096 + b * 1024:4096 + (b + 1) * 1024] for b in range(2)]
        junk_o = reg_p[:, 6144:6144 + P]
        w_sd = reg_p[:, :].rearrange("p (a j n) -> p a j n", a=2, j=4)
        ring = [reg_ka[:, 0:1024], reg_ka[:, 1024:2048], reg_g[:, 0:1024], reg_g[:, 1024:2048]]
        sg = [[early[:, (2 * b + c) * 512:(2 * b + c + 1) * 512] for c in range(2)] for b in range(2)]
        xres = [reg_p[:, i * 1024:(i + 1) * 1024] for i in range(2)]

        early_in, late_in = sem("early_in"), sem("late_in")
        x_in = [sem("x_in0"), sem("x_in1")]
        rms_ready = sem("rms_ready")
        h_ready = sem("h_ready")
        h_turned = sem("h_turned")
        hT_act, hT_dve = sem("hT_act"), sem("hT_dve")
        w_in_s = [sem("w_in0"), sem("w_in1")]
        proj_done, proj_taken = sem("proj_done"), sem("proj_taken")
        rope_ready, rope_turned, qk_stored = sem("rope_ready"), sem("rope_turned"), sem("qk_stored")
        lam_dot, lam_exp = sem("lam_dot"), sem("lam_exp")
        score_ready, max_ready, exp_ready = sem("score_ready"), sem("max_ready"), sem("exp_ready")
        mix_ready, p_turned = sem("mix_ready"), sem("p_turned")
        pT_act, pT_dve = sem("pT_act"), sem("pT_dve")
        pv_ready, o_taken = sem("pv_ready"), sem("o_taken")
        subln_rms, subln_done = sem("subln_rms"), sem("subln_done")
        o_turned, oaT_ready, obT_ready = sem("o_turned"), sem("oaT_ready"), sem("obT_ready")
        wsd_in, wo_in = sem("wsd_in"), sem("wo_in")
        gw_in = [sem(f"gw_in{i}") for i in range(4)]
        gate_ready, gate_sig, y_ready, mix_done = sem("gate_ready"), sem("gate_sig"), sem("y_ready"), sem("mix_done")
        gw_used = sem("gw_used")
        xr_in = [sem("xr_in0"), sem("xr_in1")]
        o_proj, x2_done = sem("o_proj"), sem("x2_done")
        out_s = sem("out_s")

        x_d = a["x"][0].rearrange("(t p) n -> t p n", p=P)
        w_in_d = a["w_in"][0].rearrange("(k p) n -> p k n", p=P)
        N_EARLY, N_LATE = 4 * 16, 10 * 16
        NPROJ = len(CHUNKS) * NT

        block = ctx.enter_context(nc.Block())

        @block.sync
        def _(sp):
            sp.dma_start(tabs_s[:, :], tabs_d).then_inc(early_in, 16)
            sp.dma_start(g1_b, a["attn_norm_g"][0].partition_broadcast(P)).then_inc(early_in, 16)
            for t in range(2):
                sp.dma_start(xin[t], x_d[t]).then_inc(x_in[t], 16)
            sp.dma_start(early[:, D + NCAT:], rope_d).then_inc(early_in, 16)
            sp.dma_start(bias_b, a["b_in"][0, 0:NCAT].partition_broadcast(P)).then_inc(early_in, 16)

            def load_chunk(c):
                at, n = CHUNKS[c]
                if c >= 2:
                    sp.wait_ge(proj_done, NT * (c - 1))
                sp.dma_start(wch[c % 2][:, 0:8 * n].rearrange("p (k n) -> p k n", k=KD),
                             w_in_d[:, :, at:at + n]).then_inc(w_in_s[c % 2], 16)
            load_chunk(0)
            for t in range(2, NT):
                sp.wait_ge(h_ready, t - 1)
                sp.dma_start(xin[t % 2], x_d[t]).then_inc(x_in[t % 2], 16)
            load_chunk(1)
            for n, name in enumerate(("diff_lambda_q1", "diff_lambda_k1", "diff_lambda_q2", "diff_lambda_k2")):
                sp.dma_start(lamv[:, n * HD:(n + 1) * HD], a[name][0].partition_broadcast(P)).then_inc(late_in, 16)
            sp.dma_start(subln[:, :], a["diff_subln_g"][0].partition_broadcast(P)).then_inc(late_in, 16)
            sp.dma_start(sinks, a["swa_sinks"][0].partition_broadcast(P)).then_inc(late_in, 16)
            with nc.allow_non_contiguous_dma(reason="2048 gate biases, one for a partition"):
                for n in range(4):
                    sp.dma_start(gate_bias[:, 4 * n:4 * n + 4],
                                 a["b_in"][0, C_GA + 512 * n:C_GA + 512 * (n + 1)].rearrange("(k p) -> p k", p=P)).then_inc(late_in, 16)
            for c in range(2, len(CHUNKS)):
                load_chunk(c)
            w_ga_gb = [a["w_in"][0, :, at:at + D].rearrange("(k p) n -> p k n", p=P) for at in (C_GA, C_GB)]
            sp.wait_ge(pv_ready, NU)

            def load_gate(g):
                if g >= 4:
                    sp.wait_ge(gw_used, g - 3)
                d, br = g // 2, g % 2
                sp.dma_start(ring[g % 4].rearrange("p (k n) -> p k n", k=KD),
                             w_ga_gb[br][:, :, d * P:(d + 1) * P]).then_inc(gw_in[g % 4], 16)
            for g in range(2):
                load_gate(g)
            w_swa = a["w_swa_out"][0].rearrange("(g j d) n -> g d j n", g=2, j=4)
            sp.wait_ge(o_taken, NU)
            for g in range(2):
                sp.dma_start(w_sd[64 * g:64 * g + 64, 0, :, :], w_swa[g]).then_inc(wsd_in, 16)
            sp.dma_start(w_sd[:, 1, :, :], a["w_diff_out"][0].rearrange("(j p) n -> p j n", p=P)).then_inc(wsd_in, 16)
            for g in range(2, 4):
                load_gate(g)
            sp.dma_start(wo_s, a["w_o"][0].rearrange("(k p) n -> p k n", p=P)).then_inc(wo_in, 16)
            for g in range(4, 2 * KD):
                load_gate(g)
            for t in range(NT):
                if t == 0:
                    sp.wait_ge(y_ready, 4 * KD)
                if t >= 2:
                    sp.wait_ge(x2_done, 2 * (t - 1))
                sp.dma_start(xres[t % 2], x_d[t]).then_inc(xr_in[t % 2], 16)
            if debug == "x2":
                sp.wait_ge(x2_done, 2 * NT)
                sp.dma_start(a["dbg"].rearrange("(t p) n -> p t n", p=P), x2).then_inc(out_s, 16)
                sp.wait_ge(out_s, 16)

        @block.scalar
        def _(act):
            def norm_rms(t):
                act.wait_ge(x_in[t % 2], 16 * (t // 2 + 1))
                act.activation(junk, xin[t % 2], ACT.Square, accum_out=ss1[:, t:t + 1])
                act.drain()
                act.activation(rms1[:, t:t + 1], ss1[:, t:t + 1], ACT.Sqrt, bias=eps_c, scale=1.0 / D).then_inc(rms_ready, 1)

            def store_h(t):
                act.wait_ge(h_turned, 2 * t + 1)
                act.activation(hT[:, 0:4, t * P:(t + 1) * P], bank[4 + 2 * (t % 2)][:, :].rearrange("p (k n) -> p k n", k=4),
                               ACT.Copy).then_inc(hT_act, 1)
            act.wait_ge(lam_dot, 1)

            def store_qk(n):
                c, t = divmod(n, NT)
                act.wait_ge(rope_turned, n + 1)
                b = bank[2 + n % 2]
                blk = slice(t * P, (t + 1) * P)
                if c == 1:
                    act.activation(kaT[:, blk], b[:, 0:P], ACT.Copy).then_inc(qk_stored, 1)
                else:
                    dst = {0: qaT, 2: qbT, 3: kbT}[c]
                    act.activation(dst[:, :, blk], b[:, :].rearrange("p (j n) -> p j n", j=4), ACT.Copy).then_inc(qk_stored, 1)
            for t in range(NT + 1):
                if t < NT:
                    norm_rms(t)
                if t >= 1:
                    store_h(t - 1)
                if t >= 3:
                    store_qk(t - 3)
            for n in range(NT - 2, TURNED_CHUNKS * NT):
                store_qk(n)
            act.wait_ge(lam_dot, 3)
            act.activation(lam_e, lam_s, ACT.Exp).then_inc(lam_exp, 1)

            def exps(u):
                kind, i, j = UNITS[u]
                n = len(keys_of(UNITS[u])) * P
                for c in range(2):
                    act.wait_ge(max_ready, 2 * u + c + 1)
                    if c == 0 and u >= 2:
                        act.wait_ge(p_turned, 2 * (u - 1))
                    s = 2 * (u % 2) + c
                    last = c == 1 and kind == "diff"
                    if n <= 512:
                        act.activation(probs[u % 2][c][:, 0:n], bank[2 * c][:, 0:n], ACT.Exp, bias=nm[:, s:s + 1],
                                       scale=ATT_SCALE, accum_out=lsum[:, s:s + 1]).then_inc(exp_ready, 1)
                    else:
                        for h in range(2):
                            w = min(512, n - 512 * h)
                            ins = act.activation(probs[u % 2][c][:, 512 * h:512 * h + w], bank[2 * c + h][:, 0:w], ACT.Exp,
                                                 bias=nm[:, s:s + 1], scale=ATT_SCALE,
                                                 accum_out=(lsum if h == 0 else mx)[:, s:s + 1])
                        ins.then_inc(exp_ready, 1)
                    if kind == "swa":
                        head = j + 4 * c
                        act.activation(sink_e[:, s:s + 1], sinks[:, head:head + 1], ACT.Exp, bias=nm[:, s:s + 1]).then_inc(exp_ready, 1)

            def store_p(u):
                kind = UNITS[u][0]
                n = len(keys_of(UNITS[u])) * P * (2 if kind == "swa" else 1)
                act.wait_ge(p_turned, 2 * u + 1)
                if u >= 2:
                    act.wait_ge(pv_ready, u - 1)
                w = min(n, 512)
                act.activation(pT[u % 2][:, 0:w], bank[4][:, 0:w], ACT.Copy).then_inc(pT_act, 1)
            act.wait_ge(late_in, N_LATE)
            for u in range(NU + 1):
                if u < NU:
                    exps(u)
                if u >= 1:
                    store_p(u - 1)
            act.wait_ge(o_taken, NU)
            act.activation(rmsb, ssb, ACT.Sqrt, bias=eps_c, scale=1.0 / (2 * HD)).then_inc(subln_rms, 1)
            for i in range(NT):
                act.wait_ge(o_turned, 2 * i + 1)
                act.activation(qaT[:, :, i * P:(i + 1) * P], bank[2 * (i % 2)][:, :].rearrange("p (j n) -> p j n", j=4),
                               ACT.Copy).then_inc(oaT_ready, 1)
            for s in range(4 * KD):
                d, br = s // 4, s % 2
                act.wait_ge(gate_ready, s + 1)
                if s >= 4:
                    act.wait_ge(mix_done, s // 2 - 1)
                act.activation(sg[(s // 2) % 2][br], bank[br][:, :], ACT.Sigmoid,
                               bias=gate_bias[:, 8 * br + d:8 * br + d + 1]).then_inc(gate_sig, 1)

        @block.vector
        def _(dve):
            dve.memset(eps_c, EPS).then_inc(lam_dot, 1)

            def norm(t):
                dve.wait_ge(rms_ready, t + 1)
                dve.reciprocal(rstd1[:, t:t + 1], rms1[:, t:t + 1])
                dve.drain()
                if t >= 2:
                    dve.wait_ge(h_turned, 2 * (t - 1))
                dve.scalar_tensor_tensor(out=hn[t % 2], in0=xin[t % 2], scalar=rstd1[:, t:t + 1], in1=g1_b,
                                         op0=ALU.mult, op1=ALU.mult).then_inc(h_ready, 1)

            def store_h(t):
                dve.wait_ge(h_turned, 2 * t + 2)
                dve.tensor_copy(hT[:, 4:8, t * P:(t + 1) * P],
                                bank[5 + 2 * (t % 2)][:, :].rearrange("p (k n) -> p k n", k=4)).then_inc(hT_dve, 1)
            def bias_and_rope(n):
                c, t = divmod(n, NT)
                at, w = CHUNKS[c]
                dve.wait_ge(proj_done, n + 1)
                b = bank[n % 2]
                if c == 4:
                    dve.tensor_tensor(vb[:, t, :], b[:, :], bias_b[:, at:at + w], ALU.add).then_inc(proj_taken, 1)
                    return
                w = P if c == 1 else 512
                if c == 1:
                    dve.tensor_tensor(va[:, t, :], b[:, P:2 * P], bias_b[:, at + P:at + 2 * P], ALU.add)
                x = biased[n % 2]
                dve.tensor_tensor(x[:, 0:w], b[:, 0:w], bias_b[:, at:at + w], ALU.add).then_inc(proj_taken, 1)
                dve.drain()
                heads = w // HD
                xv = x[:, 0:w].rearrange("p (h s e) -> p h s e", h=heads, s=2)
                r = rot[n % 2]
                rv = r[:, 0:w].rearrange("p (h s e) -> p h s e", h=heads, s=2)
                sv = sin_s[:, t, :].rearrange("p (s e) -> p s e", s=2)
                for h in range(2):
                    dve.tensor_tensor(rv[:, :, h, :], xv[:, :, 1 - h, :],
                                      sv[:, h, :].unsqueeze(1).to_broadcast([P, heads, HD // 2]), ALU.mult)
                dve.drain()
                dve.tensor_tensor(x[:, 0:w].rearrange("p (h e) -> p h e", h=heads), x[:, 0:w].rearrange("p (h e) -> p h e", h=heads),
                                  cos_s[:, t, :].unsqueeze(1).to_broadcast([P, heads, HD]), ALU.mult)
                dve.drain()
                if n >= 2:
                    dve.wait_ge(rope_turned, n - 1)
                o = roped[n % 2]
                if c == 0:
                    dve.tensor_tensor(o.rearrange("p (j g e) -> p g j e", j=4, g=2), x.rearrange("p (g j e) -> p g j e", g=2, j=4),
                                      r.rearrange("p (g j e) -> p g j e", g=2, j=4), ALU.add).then_inc(rope_ready, 1)
                else:
                    dve.tensor_tensor(o[:, 0:w], x[:, 0:w], r[:, 0:w], ALU.add).then_inc(rope_ready, 1)
            dve.wait_ge(early_in, N_EARLY)
            for t in range(NT + 1):
                if t < NT:
                    norm(t)
                if t >= 1:
                    store_h(t - 1)
                if t >= 2:
                    bias_and_rope(t - 2)
            for n in range(NT - 1, NPROJ):
                bias_and_rope(n)
            dve.wait_ge(late_in, N_LATE)
            for n in range(2):
                dve.tensor_tensor_reduce(junk_o[:, n * HD:(n + 1) * HD], lamv[:, 2 * n * HD:(2 * n + 1) * HD],
                                         lamv[:, (2 * n + 1) * HD:(2 * n + 2) * HD], 1.0, 0.0, ALU.mult, ALU.add,
                                         lam_s[:, n:n + 1]).then_inc(lam_dot, 1)
            dve.tensor_scalar(neg_sinks, sinks, -1.0, None, ALU.mult)
            dve.tensor_scalar(subln[:, :], subln[:, :], 1.0 - LAM_INIT, None, ALU.mult)
            dve.wait_ge(lam_exp, 1)
            dve.tensor_tensor(neg_lam, lam_e[:, 1:2], lam_e[:, 0:1], ALU.subtract)
            dve.drain()
            dve.tensor_scalar(neg_lam, neg_lam, -LAM_INIT, None, ALU.add)


            def maxima(u):
                kind, i, j = UNITS[u]
                keys = keys_of(UNITS[u])
                for c in range(2):
                    s = 2 * (u % 2) + c
                    dve.wait_ge(score_ready, 2 * u + c + 1)
                    last = len(keys) - 1
                    bk = bank[2 * c + last // 4]
                    v = bk[:, (last % 4) * P:(last % 4 + 1) * P]
                    dve.tensor_tensor(v, v, causal, ALU.add)
                    if kind == "swa" and i:
                        v = bank[2 * c][:, 0:P]
                        dve.tensor_tensor(v, v, before, ALU.add)
                    dve.drain()
                    n = len(keys) * P
                    if n <= 512:
                        dve.tensor_reduce(mx[:, s:s + 1], bank[2 * c][:, 0:n], AX.X, ALU.max)
                    else:
                        dve.tensor_reduce(mx[:, s:s + 1], bank[2 * c][:, :], AX.X, ALU.max)
                        dve.tensor_reduce(coef[:, c:c + 1], bank[2 * c + 1][:, 0:n - 512], AX.X, ALU.max)
                        dve.drain()
                        dve.tensor_tensor(mx[:, s:s + 1], mx[:, s:s + 1], coef[:, c:c + 1], ALU.max)
                    dve.drain()
                    if kind == "swa":
                        head = j + 4 * c
                        dve.tensor_scalar(nm[:, s:s + 1], mx[:, s:s + 1], -ATT_SCALE, neg_sinks[:, head:head + 1],
                                          ALU.mult, ALU.min).then_inc(max_ready, 1)
                    else:
                        dve.tensor_scalar(nm[:, s:s + 1], mx[:, s:s + 1], -ATT_SCALE, None, ALU.mult).then_inc(max_ready, 1)

            def exp_count(u):
                return 2 * u + 2 * units_before("swa", u)

            def mix(u):
                kind, i, j = UNITS[u]
                n = len(keys_of(UNITS[u])) * P
                dve.wait_ge(exp_ready, exp_count(u + 1))
                s = 2 * (u % 2)
                r = rinv[:, 2 * (u % 4):2 * (u % 4) + 2]
                if kind == "swa":
                    dve.tensor_tensor(lsum[:, s:s + 2], lsum[:, s:s + 2], sink_e[:, s:s + 2], ALU.add)
                    dve.drain()
                    dve.reciprocal(r, lsum[:, s:s + 2]).then_inc(mix_ready, 1)
                    return
                if n > 512:
                    dve.tensor_tensor(lsum[:, s:s + 2], lsum[:, s:s + 2], mx[:, s:s + 2], ALU.add)
                    dve.drain()
                dve.reciprocal(r, lsum[:, s:s + 2])
                dve.drain()
                dve.scalar_tensor_tensor(out=coef[:, 0:1], in0=lsum[:, s:s + 1], scalar=neg_lam, in1=r[:, 1:2],
                                         op0=ALU.mult, op1=ALU.mult)
                dve.drain()
                pr = probs[u % 2]
                dve.scalar_tensor_tensor(out=pr[0][:, 0:n], in0=pr[1][:, 0:n], scalar=coef[:, 0:1], in1=pr[0][:, 0:n],
                                         op0=ALU.mult, op1=ALU.add).then_inc(mix_ready, 1)

            def store_p(u):
                kind, i, j = UNITS[u]
                n = len(keys_of(UNITS[u])) * P
                if kind == "swa" or n <= 512:
                    return
                dve.wait_ge(p_turned, 2 * u + 2)
                if u >= 2:
                    dve.wait_ge(pv_ready, u - 1)
                dve.tensor_copy(pT[u % 2][:, 512:n], bank[5][:, 0:n - 512]).then_inc(pT_dve, 1)

            def finish(u):
                kind, i, j = UNITS[u]
                dve.wait_ge(pv_ready, u + 1)
                r = rinv[:, 2 * (u % 4):2 * (u % 4) + 2]
                o = bank[6 + u % 2]
                if kind == "swa":
                    for c in range(2):
                        ins = dve.tensor_scalar(oan[:, i, j, c * HD:(c + 1) * HD], o[:, c * HD:(c + 1) * HD], r[:, c:c + 1], None, ALU.mult)
                    ins.then_inc(o_taken, 1)
                else:
                    dve.tensor_scalar(obn[:, i, j, :], o[:, 0:P], r[:, 0:1], None, ALU.mult)
                    dve.drain()
                    dve.tensor_tensor_reduce(junk_o, obn[:, i, j, :], obn[:, i, j, :], 1.0, 0.0, ALU.mult, ALU.add,
                                             ssb[:, 4 * i + j:4 * i + j + 1]).then_inc(o_taken, 1)
            for u in range(NU + 2):
                if 1 <= u <= NU:
                    mix(u - 1)
                if u < NU:
                    maxima(u)
                if 1 <= u <= NU:
                    store_p(u - 1)
                if u >= 2:
                    finish(u - 2)
            dve.wait_ge(subln_rms, 1)
            dve.reciprocal(rstdb, rmsb)
            dve.drain()
            for i in range(NT):
                o = obn[:, i, :, :]
                dve.tensor_tensor(o, o, rstdb[:, 4 * i:4 * i + 4].unsqueeze(2).to_broadcast([P, 4, P]), ALU.mult)
                dve.drain()
                dve.tensor_tensor(o, o, subln[:, :].unsqueeze(1).to_broadcast([P, 4, P]), ALU.mult).then_inc(subln_done, 1)
                if i >= 1:
                    dve.wait_ge(o_turned, 2 * i)
                    dve.tensor_copy(qbT[:, :, (i - 1) * P:i * P],
                                    bank[1 + 2 * ((i - 1) % 2)][:, :].rearrange("p (j n) -> p j n", j=4)).then_inc(obT_ready, 1)
            i = NT
            dve.wait_ge(o_turned, 2 * i)
            dve.tensor_copy(qbT[:, :, (i - 1) * P:i * P],
                            bank[1 + 2 * ((i - 1) % 2)][:, :].rearrange("p (j n) -> p j n", j=4)).then_inc(obT_ready, 1)
            for m in range(2 * KD):
                d, half = m // 2, m % 2
                for br in range(2):
                    dve.wait_ge(gate_sig, 2 * m + br + 1)
                    dve.wait_ge(y_ready, 2 * m + br + 1)
                    g = sg[m % 2][br]
                    ins = dve.tensor_tensor(g, g, bank[2 + br + 2 * (m % 2)][:, :], ALU.mult)
                dve.drain()
                dve.tensor_tensor(mixT[:, d, half * 512:(half + 1) * 512], sg[m % 2][0], sg[m % 2][1], ALU.add).then_inc(mix_done, 1)
            for n in range(2 * NT):
                t, half = n // 2, n % 2
                dve.wait_ge(xr_in[t % 2], 16 * (t // 2 + 1))
                dve.wait_ge(o_proj, n + 1)
                dve.tensor_tensor(x2[:, t, half * 512:(half + 1) * 512], bank[6 + n % 2][:, :],
                                  xres[t % 2][:, half * 512:(half + 1) * 512], ALU.add).then_inc(x2_done, 1)

        @block.tensor
        def _(pe):
            pe.wait_ge(early_in, N_EARLY)

            def turn_h(t):
                pe.wait_ge(h_ready, t + 1)
                for half in range(2):
                    if t >= 2:
                        pe.wait_ge(hT_act if half == 0 else hT_dve, t - 1)
                    for k in range(4):
                        ins = pe.transpose(bank[4 + 2 * (t % 2) + half][:, k * P:(k + 1) * P],
                                           hn[t % 2][:, (4 * half + k) * P:(4 * half + k + 1) * P], ident)
                    ins.then_inc(h_turned, 1)

            def project(n):
                c, t = divmod(n, NT)
                w = CHUNKS[c][1]
                if t == 0:
                    pe.wait_ge(w_in_s[c % 2], 16 * (c // 2 + 1))
                if n >= 2:
                    pe.wait_ge(proj_taken, n - 1)
                if c == 0:
                    pe.wait_ge(hT_act, t + 1)
                    pe.wait_ge(hT_dve, t + 1)
                wv = wch[c % 2][:, 0:8 * w].rearrange("p (k n) -> p k n", k=KD)
                for k in range(KD):
                    ins = pe.matmul(bank[n % 2][:, 0:w], hT[:, k, t * P:(t + 1) * P], wv[:, k, :], start=(k == 0), stop=(k == KD - 1))
                ins.then_inc(proj_done, 1)

            def turn_rope(n):
                c, t = divmod(n, NT)
                if c >= TURNED_CHUNKS:
                    return
                pe.wait_ge(rope_ready, n + 1)
                if n >= 2:
                    pe.wait_ge(qk_stored, n - 1)
                for j in range(1 if c == 1 else 4):
                    ins = pe.transpose(bank[2 + n % 2][:, j * P:(j + 1) * P], roped[n % 2][:, j * P:(j + 1) * P], ident)
                ins.then_inc(rope_turned, 1)
            for t in range(NT):
                turn_h(t)
                if t >= 1:
                    project(t - 1)
                if t >= 2:
                    turn_rope(t - 2)
            for n in range(NT - 1, NPROJ):
                project(n)
                turn_rope(n - 1)
            turn_rope(NPROJ - 1)

            def scores(u):
                kind, i, j = UNITS[u]
                keys = keys_of(UNITS[u])
                k0, n = keys[0] * P, len(keys) * P
                if u >= 1:
                    pe.wait_ge(exp_ready, 2 * u + 2 * units_before("swa", u))
                for c in range(2):
                    q = (qaT if kind == "swa" else qbT)[64 * c:64 * c + 64, j, i * P:(i + 1) * P]
                    kk = (kaT[64 * c:64 * c + 64, :] if kind == "swa" else kbT[64 * c:64 * c + 64, j, :])
                    for h in range(0, n, 512):
                        w = min(512, n - h)
                        ins = pe.matmul(bank[2 * c + h // 512][:, 0:w], q, kk[:, k0 + h:k0 + h + w], start=True, stop=True)
                    ins.then_inc(score_ready, 1)

            def turn_p(u):
                kind, i, j = UNITS[u]
                n = len(keys_of(UNITS[u]))
                pe.wait_ge(mix_ready, u + 1)
                if u >= 1:
                    pe.wait_ge(pT_act, u)
                    done = sum(1 for x in UNITS[:u] if x[0] == "diff" and len(keys_of(x)) > 4)
                    if done:
                        pe.wait_ge(pT_dve, done)
                tiles = [(c, m) for c in range(2) for m in range(n)] if kind == "swa" else [(0, m) for m in range(n)]
                for at, (c, m) in enumerate(tiles):
                    ins = pe.transpose(bank[4 + at // 4][:, (at % 4) * P:(at % 4 + 1) * P],
                                       probs[u % 2][c][:, m * P:(m + 1) * P], ident)
                    if at == min(3, len(tiles) - 1):
                        ins.then_inc(p_turned, 1)
                        ins = None
                if ins is None:
                    pe.drain()
                    pe.sem_inc(p_turned, 1)
                else:
                    ins.then_inc(p_turned, 1)

            def product(u):
                kind, i, j = UNITS[u]
                keys = keys_of(UNITS[u])
                pe.wait_ge(pT_act, u + 1)
                done = sum(1 for x in UNITS[:u + 1] if x[0] == "diff" and len(keys_of(x)) > 4)
                if done:
                    pe.wait_ge(pT_dve, done)
                if u >= 2:
                    pe.wait_ge(o_taken, u - 1)
                o = bank[6 + u % 2]
                if kind == "swa":
                    for c in range(2):
                        for m, kt in enumerate(keys):
                            at = c * len(keys) + m
                            ins = pe.matmul(o[:, c * HD:(c + 1) * HD], pT[u % 2][:, at * P:(at + 1) * P],
                                            va[:, kt, c * HD:(c + 1) * HD], start=(m == 0), stop=(m == len(keys) - 1))
                else:
                    for m, kt in enumerate(keys):
                        ins = pe.matmul(o[:, 0:P], pT[u % 2][:, m * P:(m + 1) * P], vb[:, kt, j * P:(j + 1) * P],
                                        start=(m == 0), stop=(m == len(keys) - 1))
                ins.then_inc(pv_ready, 1)
            pe.wait_ge(qk_stored, TURNED_CHUNKS * NT)
            pe.wait_ge(proj_taken, NPROJ)
            for u in range(NU + 2):
                if u < NU:
                    scores(u)
                if 1 <= u <= NU:
                    turn_p(u - 1)
                if u >= 2:
                    product(u - 2)
            for i in range(NT):
                if i >= 2:
                    pe.wait_ge(oaT_ready, i - 1)
                else:
                    pe.wait_ge(o_taken, NU)
                for j in range(4):
                    ins = pe.transpose(bank[2 * (i % 2)][:, j * P:(j + 1) * P], oan[:, i, j, :], ident)
                ins.then_inc(o_turned, 1)
                pe.wait_ge(subln_done, i + 1)
                if i >= 2:
                    pe.wait_ge(obT_ready, i - 1)
                for j in range(4):
                    ins = pe.transpose(bank[1 + 2 * (i % 2)][:, j * P:(j + 1) * P], obn[:, i, j, :], ident)
                ins.then_inc(o_turned, 1)
            pe.wait_ge(wsd_in, 48)
            pe.wait_ge(oaT_ready, NT)
            pe.wait_ge(obT_ready, NT)
            for m in range(2 * KD):
                d, half = m // 2, m % 2
                tok = slice(half * 512, (half + 1) * 512)
                for br in range(2):
                    g = 2 * d + br
                    if half == 0:
                        pe.wait_ge(gw_in[g % 4], 16 * (g // 4 + 1))
                    if m >= 1:
                        pe.wait_ge(gate_sig, 2 * m + br - 1)
                    wv = ring[g % 4].rearrange("p (k n) -> p k n", k=KD)
                    for k in range(KD):
                        ins = pe.matmul(bank[br][:, :], wv[:, k, :], hT[:, k, tok], start=(k == 0), stop=(k == KD - 1))
                    ins.then_inc(gate_ready, 1)
                for br in range(2):
                    if m >= 2:
                        pe.wait_ge(mix_done, m - 1)
                    oT = (qaT, qbT)[br]
                    for j in range(4):
                        ins = pe.matmul(bank[2 + br + 2 * (m % 2)][:, :], w_sd[:, br, j, d * P:(d + 1) * P], oT[:, j, tok],
                                        start=(j == 0), stop=(j == 3))
                    ins.then_inc(y_ready, 1)
                if half == 1:
                    pe.drain()
                    pe.sem_inc(gw_used, 2)
            pe.wait_ge(wo_in, 16)
            pe.wait_ge(mix_done, 2 * KD)
            for n in range(2 * NT):
                t, half = n // 2, n % 2
                if n >= 2:
                    pe.wait_ge(x2_done, n - 1)
                for k in range(KD):
                    ins = pe.matmul(bank[6 + n % 2][:, :], mixT[:, k, t * P:(t + 1) * P], wo_s[:, k, half * 512:(half + 1) * 512],
                                    start=(k == 0), stop=(k == KD - 1))
                ins.then_inc(o_proj, 1)


CAP = 384
CT = CAP // P
VARIANTS = [64, 128, 192, 256, 320, 384]
EXTRA = NEXP + (S * TOPK) // (CAP + 1)
NLIST = 48
CANDS = 2 * NEXP
ROWS = S + CAP
PIECES = 4
PC = FF // PIECES
SWIGLU_LIMIT, SWIGLU_ALPHA = 7.0, 1.702


def expert_constants():
    p = np.arange(P)
    f = np.zeros((P, 640), np.float32)
    f[:, 0:CAP] = np.arange(CAP)[None, :]
    f[:, 384:387] = S + p[:, None] + P * np.arange(CT)[None, :]
    f[:CANDS, 387] = CAP * (1 + p[:CANDS] // NEXP)
    f[:CANDS, 388] = p[:CANDS] % NEXP
    f[:, 389] = 1.0
    f[:CANDS, 400:464] = (p[:CANDS, None] < p[None, :CANDS])
    f[:, 464:592] = 1.0
    b = np.zeros((P, 256 + 8 * 6 + 1), np.float32)
    b[:, 0:128] = (p[:, None] < p[None, :])
    b[:, 128:256] = 1.0
    g = b[:, 256:304].reshape(P, 8, 6)
    g[:, :, 0] = np.arange(8)[None, :]
    g[:, :, 1] = p[:, None]
    g[:, :, 2] = 1.0
    b[:, 304] = 1.0
    return f, b


def expert_half(nc, a, tabs_s, reg_h, debug=None):
    fc, bc = expert_constants()
    fc_d = nc.inline_tensor(fc, name="slot_table").ap()
    bc_d = nc.inline_tensor(bc, name="order_table").ap()
    ident = tabs_s[:, 0:P]
    xn_d = nc.dram_tensor("xn_rows", [ROWS, D], F32, kind="Internal").ap()
    acc_d = nc.dram_tensor("acc_rows", [ROWS, D], F32, kind="Internal").ap()
    with ExitStack() as ctx:
        def sb(name, shape, dt=F32):
            return ctx.enter_context(nc.sbuf_tensor(name, shape, dt))

        def sem(name):
            return ctx.enter_context(nc.semaphore(name))

        bank = [ctx.enter_context(nc.psum_tensor(f"xbank{i}", [P, 512], F32)) for i in range(8)]
        x2 = reg_h[:, :].rearrange("p (t n) -> p t n", t=NT)
        w1r = sb("w1r", [P, PIECES, KD, 2, PC])
        w2r = sb("w2r", [P, PIECES, KD, PC])
        xg = sb("xg", [P, CT, D])
        xT = sb("xT", [P, KD, CAP])
        actT = sb("actT", [P, KD, CAP])
        yT = sb("yT", [P, KD, CAP])
        yrow = sb("yrow", [P, CT, D])
        b1T = sb("b1T", [P, NEXP, 2 * KD])
        rankm = sb("rankm", [P, NEXP, NT])
        gparts = sb("gparts", [P, NEXP, NT, 3], BF16)
        fcs = sb("fcs", [P, 640])
        bcs = sb("bcs", [P, 305], BF16)
        lists = sb("lists", [P, 3, NLIST])
        listi = sb("listi", [P, 3, NLIST], I32)
        nitem = sb("nitem", [P, 1], I32)
        sm = sb("sm", [P, 512])
        onehot = reg_h[:, 0:CAP * NT // 2].bitcast(BF16).rearrange("p (t s) -> p t s", t=NT)
        at = CAP * NT // 2
        gl = [reg_h[:, at + n * CAP:at + (n + 1) * CAP] for n in range(2)]
        ul = [reg_h[:, at + (2 + n) * CAP:at + (3 + n) * CAP] for n in range(2)]
        sg = [reg_h[:, at + (4 + n) * CAP:at + (5 + n) * CAP] for n in range(2)]
        xgf, xTf, actf, yTf, yrf = (v[:, :, :].rearrange("p a b -> p (a b)") for v in (xg, xT, actT, yT, yrow))
        xn = [xgf[:, 0:D], xgf[:, D:2 * D]]
        g2_b = xgf[:, 2 * D:3 * D]
        xnT = [xTf[:, n * D:(n + 1) * D].rearrange("p (k s) -> p k s", k=KD) for n in range(2)]
        junk = xTf[:, 2 * D:3 * D]
        b1n = actf[0:NEXP, 0:2 * FF]
        rw = actf[:, 2 * FF:2 * FF + 256].rearrange("p (k e) -> p k e", k=KD)
        rb_b = actf[:, 2 * FF + 256:2 * FF + 288]
        b2n = yTf[0:NEXP, 0:D]
        gT = yTf[0:NEXP, D:2 * D]
        zero = yTf[:, 2 * D:3 * D]
        lg = yrf[:, 0:256].rearrange("p (t e) -> p t e", t=NT)
        gates = yrf[:, 256:512].rearrange("p (t e) -> p t e", t=NT)
        hot = yrf[:, 512:640].rearrange("p (k e) -> p k e", k=TOPK)
        maskf = yrf[:, 640:896].rearrange("p (t e) -> p t e", t=NT)
        maskb = yrf[:, 896:1152].bitcast(BF16).rearrange("p (t e) -> p t e", t=NT)
        gres = yrf[:, 1152:1408].rearrange("p (e t) -> p e t", t=NT)
        gres2 = yrf[:, 1408:1664].rearrange("p (e t) -> p e t", t=NT)
        cand_v = yrf[:, 1664:1664 + 3 * P].rearrange("p (v n) -> p v n", v=3)
        cand_hot = yrf[:, 2048:2048 + NLIST - NEXP]
        iota_e = fcs[:, 0:NEXP]
        iota_s = fcs[:, 0:CAP]
        unused_row = fcs[:, 384:387]
        cand_first, cand_exp = fcs[0:CANDS, 387:388], fcs[0:CANDS, 388:389]
        cand_before = fcs[0:CANDS, 400:464]
        ones_f = fcs[:, 464:592]
        tri, ones_b = bcs[:, 0:P], bcs[:, P:2 * P]
        gcur = bcs[:, 256:304].rearrange("p (t v) -> p t v", t=NT)
        one_b = bcs[:, 304:305]
        eps_c = sm[:, 0:1]
        ss2, rms2, rstd2 = sm[:, 8:16], sm[:, 16:24], sm[:, 24:32]
        top = sm[:, 32:96].rearrange("p (t k) -> p t k", t=NT)
        topi = sm[:, 96:160].bitcast(U32).rearrange("p (t k) -> p t k", t=NT)
        topf = sm[:, 160:192].rearrange("p (t k) -> p t k", t=NT)
        ex = sm[:, 192:224].rearrange("p (t k) -> p t k", t=NT)
        ntop, exs, rexs = sm[:, 224:232], sm[:, 232:240], sm[:, 240:248]
        cand_n, cand_flag, cand_pos = sm[0:CANDS, 248:249], sm[0:CANDS, 249:250], sm[0:CANDS, 250:251]
        rk, rk0, basec = sm[:, 256:264], sm[:, 264:272], sm[:, 272:273]
        b1c = [sm[:, 280 + 16 * n:296 + 16 * n] for n in range(2)]
        idxf, padf = sm[:, 320:323], sm[:, 324:327]
        idxg, gateg = sm[:, 328:331].bitcast(I32), sm[:, 332:335]
        idxs, gates_s = sm[:, 336:339].bitcast(I32), sm[:, 340:343]
        ss3, rms3, rstd3 = sm[:, 352:360], sm[:, 360:368], sm[:, 368:376]
        spare = sm[0:1, 384:400]

        route_in, xn_out, acc_out, zero_out = sem("route_in"), [sem("xn_out0"), sem("xn_out1")], sem("acc_out"), sem("zero_out")
        setup, order_in = sem("setup"), sem("order_in")
        rms2_ready, xn_ready, xn_turned, xnT_act, xnT_dve = (sem(n) for n in ("rms2_ready", "xn_ready", "xn_turned", "xnT_act", "xnT_dve"))
        logits_done, logits_taken, top_ready, ex_ready, mask_ready = (sem(n) for n in ("logits_done", "logits_taken", "top_ready", "ex_ready", "mask_ready"))
        count_done, flag_ready, pos_done, cand_ready, list_done, list_ready = (
            sem(n) for n in ("count_done", "flag_ready", "pos_done", "cand_ready", "list_done", "list_ready"))
        gt_done, gt_taken, b2_done, acc_ready = (sem(n) for n in ("gt_done", "gt_taken", "b2_done", "acc_ready"))
        b1_turned, b1_taken = sem("b1_turned"), sem("b1_taken")
        w1_in = [sem(f"w1_in{q}") for q in range(PIECES)]
        w2_in = [sem(f"w2_in{q}") for q in range(PIECES)]
        w1_used, w2_used = sem("w1_used"), sem("w2_used")
        hot_ready, slots_done, slots_ready = sem("hot_ready"), sem("slots_done"), sem("slots_ready")
        rows_in, waits_taken = sem("rows_in"), sem("waits_taken")
        x_turned, xT_ready = sem("x_turned"), sem("xT_ready")
        up_done, up_taken, gate_ready, sig_ready, act_ready = (sem(n) for n in ("up_done", "up_taken", "gate_min", "sig_ready", "act_ready"))
        down_done, down_taken = sem("down_done"), sem("down_taken")
        y_turned, yrow_act, yrow_dve, sslots_ready, rows_added = (
            sem(n) for n in ("y_turned", "yrow_act", "yrow_dve", "sslots_ready", "rows_added"))
        f_g = sem("f_g")
        f_in, f_rms, f_ready, f_out = [sem("f_in0"), sem("f_in1")], sem("f_rms"), sem("f_ready"), [sem("f_out0"), sem("f_out1")]

        def by_slots(eng, count, body):
            def choose(vs):
                if len(vs) == 1:
                    body(vs[0])
                    return
                half = (len(vs) + 1) // 2
                with eng.If(count <= vs[half - 1]):
                    choose(vs[:half])
                with eng.Else():
                    choose(vs[half:])
            choose(VARIANTS)

        def by_tiles(eng, count, body):
            with eng.If(count <= P):
                body(1)
            with eng.Else():
                with eng.If(count <= 2 * P):
                    body(2)
                with eng.Else():
                    body(3)

        def item(eng, what, i):
            return eng.value_load(listi[0:1, what, bass.ds(i, 1)], min_val=0, max_val=(NEXP - 1, CAP)[what])

        def items(eng):
            eng.wait_ge(list_ready, 1)
            return eng.value_load(nitem[0:1, 0:1], min_val=NEXP, max_val=EXTRA)

        w1_d = a["w1"][0].rearrange("e (k p) (h q c) -> e q p k h c", p=P, h=2, q=PIECES)
        w2_d = a["w2"][0].rearrange("e (k p) (q c) -> e q p k c", p=P, q=PIECES)
        fin_d = a["out"][0].rearrange("(t p) n -> t p n", p=P)

        block = ctx.enter_context(nc.Block())

        @block.sync
        def _(sp):
            sp.dma_start(fcs[:, :], fc_d).then_inc(route_in, 16)
            sp.dma_start(g2_b, a["ffn_norm_g"][0].partition_broadcast(P)).then_inc(route_in, 16)
            sp.dma_start(rw, a["router_w"][0].rearrange("(k p) e -> p k e", p=P)).then_inc(route_in, 16)
            sp.dma_start(rb_b, a["router_b"][0].partition_broadcast(P)).then_inc(route_in, 16)
            sp.dma_start(b1n, a["b1"][0]).then_inc(route_in, 16)
            sp.dma_start(b2n, a["b2"][0]).then_inc(route_in, 16)
            for q in range(PIECES):
                for half in range(2):
                    sp.dma_start(w1r[:, q, :, half, :], w1_d[0, q, :, :, half, :]).then_inc(w1_in[q], 16)
            for q in range(PIECES):
                sp.dma_start(w2r[:, q, :, :], w2_d[0, q]).then_inc(w2_in[q], 16)
            for t in range(NT):
                sp.wait_ge(xn_ready, t + 1)
                sp.dma_start(xn_d[t * P:(t + 1) * P, :], xn[t % 2]).then_inc(xn_out[t % 2], 16)
            sp.wait_ge(setup, 2)
            for m in range(CT):
                sp.dma_start(xn_d[S + m * P:S + (m + 1) * P, :], zero).then_inc(zero_out, 16)
                sp.dma_start(acc_d[S + m * P:S + (m + 1) * P, :], zero).then_inc(zero_out, 16)
            for t in range(NT):
                sp.wait_ge(acc_ready, 2 * (t + 1))
                sp.dma_start(acc_d[t * P:(t + 1) * P, :], x2[:, t, :]).then_inc(acc_out, 16)
            n_items = items(sp)
            with sp.Fori(0, EXTRA - 1) as i:
                with sp.If(i + 1 < n_items):
                    e = item(sp, 0, i + 1)
                    for q in range(PIECES):
                        sp.wait_ge(w1_used, i * PIECES + (q + 1))
                        for half in range(2):
                            sp.dma_start(w1r[:, q, :, half, :],
                                         w1_d[bass.ds(e, 1), q, :, :, half, :].rearrange("o p k c -> (o p) k c")).then_inc(w1_in[q], 16)
                    for q in range(PIECES):
                        sp.wait_ge(w2_used, i * PIECES + (q + 1))
                        sp.dma_start(w2r[:, q, :, :], w2_d[bass.ds(e, 1), q].rearrange("o p k c -> (o p) k c")).then_inc(w2_in[q], 16)
            sp.wait_ge(rows_added, n_items * (16 * CT))
            sp.dma_start(yrow[:, 2, :], a["final_norm_g"].partition_broadcast(P)).then_inc(f_g, 16)
            for t in range(NT):
                if t >= 2:
                    sp.wait_ge(f_ready, t - 1)
                sp.dma_start(xg[:, t % 2, :], acc_d[t * P:(t + 1) * P, :]).then_inc(f_in[t % 2], 16)
                if t >= 1:
                    sp.wait_ge(f_ready, t)
                    sp.dma_start(fin_d[t - 1], yrow[:, (t - 1) % 2, :]).then_inc(f_out[(t - 1) % 2], 16)
            sp.wait_ge(f_ready, NT)
            sp.dma_start(fin_d[NT - 1], yrow[:, (NT - 1) % 2, :]).then_inc(f_out[(NT - 1) % 2], 16)
            for n in range(2):
                sp.wait_ge(f_out[n], 16 * NT // 2)

        @block.gpsimd
        def _(pool):
            pool.dma_start(bcs[:, :], bc_d).then_inc(order_in, 16)

            def take_waits(before):
                pool.wait_ge(waits_taken, before)
                pool.tensor_tensor(spare[:, 8:9], fcs[0:1, 0:1], fcs[0:1, 1:2], ALU.add).then_inc(waits_taken, 1)
            pool.memset(spare[:, 8:9], 0.0).then_inc(waits_taken, 1)

            def gather(i_next):
                pool.wait_ge(slots_ready, i_next + 1)
                n = item(pool, 1, i_next)

                def rows(tiles):
                    if not (isinstance(i_next, int) and i_next == 0):
                        pool.wait_ge(x_turned, CT * 2 * i_next)
                        take_waits(2 * i_next - 1)
                    for m in range(tiles):
                        pool.indirect_dma_start(out=xg[:, m, :], out_offset=None, in_=xn_d,
                                                in_offset=bass.IndirectOffsetOnAxis(ap=idxg[:, m:m + 1].bitcast(U32), axis=0)).then_inc(rows_in, 16)
                    for m in range(tiles, CT):
                        pool.dma_start(spare[:, m:m + 1], fcs[0:1, m:m + 1]).then_inc(rows_in, 16)
                by_tiles(pool, n, rows)

            def scatter(i):
                n = item(pool, 1, i)

                def rows(tiles):
                    pool.wait_ge(sslots_ready, i + 1)
                    pool.wait_ge(yrow_act, CT * (i + 1))
                    pool.wait_ge(yrow_dve, CT * (i + 1))
                    take_waits(2 * i + 2)
                    for m in range(tiles):
                        pool.indirect_dma_start(out=acc_d, out_offset=bass.IndirectOffsetOnAxis(ap=idxs[:, m:m + 1].bitcast(U32), axis=0),
                                                in_=yrow[:, m, :], in_offset=None, compute_op=ALU.add).then_inc(rows_added, 16)
                    for m in range(tiles, CT):
                        pool.dma_start(spare[:, 4 + m:5 + m], fcs[0:1, m:m + 1]).then_inc(rows_added, 16)
                by_tiles(pool, n, rows)
            n_items = items(pool)
            for n in range(2):
                pool.wait_ge(xn_out[n], 16 * NT // 2)
            pool.wait_ge(zero_out, 32 * CT)
            pool.wait_ge(acc_out, 16 * NT)
            gather(0)
            with pool.Fori(0, EXTRA) as i:
                with pool.If(i < n_items):
                    gather(i + 1)
                    scatter(i)

        @block.scalar
        def _(act):
            act.wait_ge(setup, 1)

            def norm_rms(t):
                act.activation(junk, x2[:, t, :], ACT.Square, accum_out=ss2[:, t:t + 1])
                act.drain()
                act.activation(rms2[:, t:t + 1], ss2[:, t:t + 1], ACT.Sqrt, bias=eps_c, scale=1.0 / D).then_inc(rms2_ready, 1)

            def store_xn(t):
                act.wait_ge(xn_turned, 2 * t + 1)
                if t >= 2:
                    act.wait_ge(logits_done, t - 1)
                act.activation(xnT[t % 2][:, 0:4, :], bank[4 + 2 * (t % 2)][:, :].rearrange("p (k n) -> p k n", k=4), ACT.Copy).then_inc(xnT_act, 1)
            for t in range(NT):
                norm_rms(t)
                if t >= 1:
                    store_xn(t - 1)
            store_xn(NT - 1)
            for t in range(NT):
                act.wait_ge(top_ready, t + 1)
                act.activation(ex[:, t, :], top[:, t, 0:TOPK], ACT.Exp, bias=ntop[:, t:t + 1], accum_out=exs[:, t:t + 1]).then_inc(ex_ready, 1)
            act.wait_ge(b1_turned, 1)
            act.activation(b1T[:, :, :].rearrange("p e f -> p f e"), bank[3][:, :].rearrange("p (f e) -> p f e", f=2 * KD), ACT.Copy).then_inc(b1_taken, 1)
            act.wait_ge(gt_done, 1)
            act.activation(gT[:, 0:512], bank[4][0:NEXP, :], ACT.Copy)
            act.activation(gT[:, 512:1024], bank[5][0:NEXP, :], ACT.Copy).then_inc(gt_taken, 1)
            act.wait_ge(b2_done, 2 * NT)

            def turn_x(i_next):
                n = item(act, 1, i_next)

                def tiles(nt):
                    for m in range(nt):
                        act.wait_ge(x_turned, i_next * 2 * CT + (2 * m + 1))
                        act.activation(xT[:, 0:4, m * P:(m + 1) * P], bank[6][:, :].rearrange("p (k n) -> p k n", k=4), ACT.Copy).then_inc(xT_ready, 1)
                    if nt < CT:
                        act.sem_inc(xT_ready, CT - nt)
                by_tiles(act, n, tiles)

            def sigmoids(i):
                n = item(act, 1, i)

                def body(nv):
                    for f in range(KD):
                        act.wait_ge(gate_ready, i * KD + (f + 1))
                        act.activation(sg[f % 2][:, 0:nv], gl[f % 2][:, 0:nv], ACT.Sigmoid, scale=SWIGLU_ALPHA).then_inc(sig_ready, 1)
                by_slots(act, n, body)

            def store_y(i):
                n = item(act, 1, i)

                def body(nv):
                    for d in range(KD):
                        act.wait_ge(down_done, i * KD + (d + 1))
                        act.activation(yT[:, d, 0:nv], bank[4 + d % 2][:, 0:nv], ACT.Copy).then_inc(down_taken, 1)
                by_slots(act, n, body)

            def weigh_y(i):
                n = item(act, 1, i)

                def tiles(nt):
                    act.wait_ge(sslots_ready, i + 1)
                    for m in range(nt):
                        act.wait_ge(y_turned, i * 2 * CT + (2 * m + 1))
                        act.activation(yrow[:, m, 0:512], bank[6][:, :], ACT.Copy, scale=gates_s[:, m:m + 1]).then_inc(yrow_act, 1)
                    if nt < CT:
                        act.sem_inc(yrow_act, CT - nt)
                by_tiles(act, n, tiles)
            n_items = items(act)
            turn_x(0)
            with act.Fori(0, EXTRA) as i:
                with act.If(i < n_items):
                    sigmoids(i)
                    store_y(i)
                    turn_x(i + 1)
                    weigh_y(i)
            act.wait_ge(f_in[0], 16)
            for t in range(NT):
                act.wait_ge(f_in[t % 2], 16 * (t // 2 + 1))
                act.activation(actf[:, 0:D], xg[:, t % 2, :], ACT.Square, accum_out=ss3[:, t:t + 1])
                act.drain()
                act.activation(rms3[:, t:t + 1], ss3[:, t:t + 1], ACT.Sqrt, bias=eps_c, scale=1.0 / D).then_inc(f_rms, 1)

        @block.vector
        def _(dve):
            dve.memset(eps_c, EPS).then_inc(setup, 1)
            dve.memset(zero, 0.0).then_inc(setup, 1)
            dve.wait_ge(route_in, 6 * 16)
            dve.wait_ge(order_in, 16)

            def norm(t):
                dve.wait_ge(rms2_ready, t + 1)
                dve.reciprocal(rstd2[:, t:t + 1], rms2[:, t:t + 1])
                dve.drain()
                if t >= 2:
                    dve.wait_ge(xn_turned, 2 * (t - 1))
                    dve.wait_ge(xn_out[t % 2], 16 * (t // 2))
                dve.scalar_tensor_tensor(out=xn[t % 2], in0=x2[:, t, :], scalar=rstd2[:, t:t + 1], in1=g2_b,
                                         op0=ALU.mult, op1=ALU.mult).then_inc(xn_ready, 1)

            def store_xn(t):
                dve.wait_ge(xn_turned, 2 * t + 2)
                if t >= 2:
                    dve.wait_ge(logits_done, t - 1)
                dve.tensor_copy(xnT[t % 2][:, 4:8, :], bank[5 + 2 * (t % 2)][:, :].rearrange("p (k n) -> p k n", k=4)).then_inc(xnT_dve, 1)

            def best(t):
                dve.wait_ge(logits_done, t + 1)
                dve.tensor_tensor(lg[:, t, :], bank[t % 2][:, 0:NEXP], rb_b, ALU.add).then_inc(logits_taken, 1)
                dve.drain()
                dve.max(top[:, t, :], lg[:, t, :])
                dve.drain()
                dve.max_index(topi[:, t, :], top[:, t, :], lg[:, t, :])
                dve.tensor_scalar(ntop[:, t:t + 1], top[:, t, 0:1], -1.0, None, ALU.mult)
                dve.drain()
                dve.tensor_copy(topf[:, t, :], topi[:, t, 0:TOPK]).then_inc(top_ready, 1)

            def gate(t):
                dve.wait_ge(ex_ready, t + 1)
                dve.reciprocal(rexs[:, t:t + 1], exs[:, t:t + 1])
                dve.drain()
                dve.tensor_scalar(ex[:, t, :], ex[:, t, :], rexs[:, t:t + 1], None, ALU.mult)
                for k in range(TOPK):
                    dve.tensor_scalar(hot[:, k, :], iota_e, topf[:, t, k:k + 1], None, ALU.is_equal)
                dve.drain()
                dve.tensor_tensor(maskf[:, t, :], hot[:, 0, :], hot[:, 1, :], ALU.add)
                dve.tensor_scalar(gates[:, t, :], hot[:, 0, :], ex[:, t, 0:1], None, ALU.mult)
                for k in range(1, TOPK):
                    dve.drain()
                    if k >= 2:
                        dve.tensor_tensor(maskf[:, t, :], maskf[:, t, :], hot[:, k, :], ALU.add)
                    dve.scalar_tensor_tensor(out=gates[:, t, :], in0=hot[:, k, :], scalar=ex[:, t, k:k + 1], in1=gates[:, t, :],
                                             op0=ALU.mult, op1=ALU.add)
                dve.drain()
                dve.tensor_copy(maskb[:, t, 0:NEXP], maskf[:, t, :])
                dve.tensor_copy(maskb[:, t, NEXP:CANDS], maskf[:, t, :]).then_inc(mask_ready, 1)
            for t in range(NT + 2):
                if t < NT:
                    norm(t)
                if 1 <= t <= NT:
                    store_xn(t - 1)
                if t >= 2:
                    best(t - 2)
            for t in range(NT):
                gate(t)
            gv = gates.rearrange("p t e -> p e t")
            dve.tensor_copy(gparts[:, :, :, 0], gv)
            dve.drain()
            dve.tensor_tensor(gres, gv, gparts[:, :, :, 0], ALU.subtract)
            dve.drain()
            dve.tensor_copy(gparts[:, :, :, 1], gres)
            dve.drain()
            dve.tensor_tensor(gres2, gres, gparts[:, :, :, 1], ALU.subtract)
            dve.drain()
            dve.tensor_copy(gparts[:, :, :, 2], gres2)
            dve.wait_ge(count_done, 1)
            rv = rankm[:, :, :].rearrange("p e t -> p t e")
            dve.tensor_scalar(rv, bank[2][:, 0:256].rearrange("p (t e) -> p t e", t=NT), 1.0, None, ALU.add)
            dve.drain()
            dve.tensor_tensor(rv, rv, maskf, ALU.mult)
            dve.drain()
            dve.tensor_scalar(rankm[:, :, :], rankm[:, :, :], -1.0, None, ALU.add)
            dve.memset(lists[:, :, :], 0.0)
            dve.drain()
            dve.tensor_copy(lists[:, 0, 0:NEXP], iota_e)
            dve.tensor_scalar(lists[:, 1, 0:NEXP], bank[2][:, 256:256 + NEXP], float(CAP), None, ALU.min)
            dve.tensor_copy(cand_n, bank[2][0:CANDS, 300:301])
            dve.drain()
            dve.tensor_tensor(cand_flag, cand_n, cand_first, ALU.is_gt)
            dve.tensor_scalar(cand_v[0:CANDS, 0, :], ones_f[0:CANDS, :], cand_exp, None, ALU.mult)
            dve.tensor_scalar(cand_v[0:CANDS, 2, :], ones_f[0:CANDS, :], cand_first, None, ALU.mult)
            dve.tensor_scalar(cand_n, cand_n, cand_first, float(CAP), ALU.subtract, ALU.min)
            dve.drain()
            dve.tensor_scalar(cand_v[0:CANDS, 1, :], ones_f[0:CANDS, :], cand_n, None, ALU.mult).then_inc(flag_ready, 1)
            dve.wait_ge(pos_done, 1)
            dve.tensor_copy(cand_pos, bank[0][0:CANDS, 0:1])
            dve.tensor_scalar(nitem[:, :], bank[0][:, 1:2], float(NEXP), None, ALU.add)
            dve.drain()
            dve.tensor_scalar(cand_hot[0:CANDS, :], iota_e[0:CANDS, 0:NLIST - NEXP], cand_pos, cand_flag, ALU.is_equal, ALU.mult).then_inc(cand_ready, 1)
            dve.wait_ge(list_done, 1)
            dve.tensor_copy(lists[:, :, NEXP:NLIST], bank[1][:, 0:3 * (NLIST - NEXP)].rearrange("p (v n) -> p v n", v=3))
            dve.drain()
            dve.tensor_copy(listi[:, :, :], lists[:, :, :]).then_inc(list_ready, 1)
            for n in range(2 * NT):
                t, half = n // 2, n % 2
                dve.wait_ge(b2_done, n + 1)
                v = x2[:, t, half * 512:(half + 1) * 512]
                dve.tensor_tensor(v, v, bank[6 + n % 2][:, :], ALU.add).then_inc(acc_ready, 1)
            dve.wait_ge(acc_out, 16 * NT)
            dve.wait_ge(b1_taken, 1)
            dve.wait_ge(zero_out, 32 * CT)
            dve.memset(yT[:, :, :], 0.0)

            def slots(i_next, cond=None):
                e = item(dve, 0, i_next)
                dve.tensor_copy(rk0, rankm[:, bass.ds(e, 1), :].rearrange("p o t -> p (o t)"))
                dve.tensor_copy(basec, lists[:, 2, bass.ds(i_next, 1)])
                dve.tensor_copy(gcur[:, :, 3:6], gparts[:, bass.ds(e, 1), :, :].rearrange("p o t v -> p (o t) v"))
                dve.tensor_copy(b1c[0], b1T[:, bass.ds(e, 1), :].rearrange("p o f -> p (o f)"))
                dve.drain()
                dve.tensor_scalar(rk, rk0, basec, None, ALU.subtract)
                dve.drain()
                for t in range(NT):
                    ins = dve.tensor_scalar(onehot[:, t, :], iota_s, rk[:, t:t + 1], None, ALU.is_equal)
                ins.then_inc(hot_ready, 1)

            def read_slots(i_next):
                dve.wait_ge(slots_done, i_next + 1)
                v = bank[7][:, 0:CT * 6].rearrange("p (m v) -> p m v", m=CT)
                dve.tensor_scalar(padf, v[:, :, 2], -1.0, 1.0, ALU.mult, ALU.add)
                dve.tensor_scalar(idxf, v[:, :, 0], float(P), None, ALU.mult)
                dve.tensor_copy(gateg, v[:, :, 3])
                dve.drain()
                dve.tensor_tensor(padf, padf, unused_row, ALU.mult)
                dve.tensor_tensor(idxf, idxf, v[:, :, 1], ALU.add)
                dve.tensor_tensor(gateg, gateg, v[:, :, 4], ALU.add)
                dve.drain()
                dve.tensor_tensor(gateg, gateg, v[:, :, 5], ALU.add)
                dve.tensor_tensor(idxf, idxf, padf, ALU.add)
                dve.drain()
                if not (isinstance(i_next, int) and i_next == 0):
                    dve.wait_ge(rows_in, 16 * CT * i_next)
                dve.tensor_copy(idxg, idxf).then_inc(slots_ready, 1)

            def turn_x(i_next):
                n = item(dve, 1, i_next)

                def tiles(nt):
                    for m in range(nt):
                        dve.wait_ge(x_turned, i_next * 2 * CT + (2 * m + 2))
                        dve.tensor_copy(xT[:, 4:8, m * P:(m + 1) * P], bank[7][:, :].rearrange("p (k n) -> p k n", k=4)).then_inc(xT_ready, 1)
                    if nt < CT:
                        dve.sem_inc(xT_ready, CT - nt)
                by_tiles(dve, n, tiles)

            def swiglu(i):
                n = item(dve, 1, i)

                def body(nv):
                    for f in range(KD):
                        b = 2 * (f % 2)
                        g, u, s = gl[f % 2][:, 0:nv], ul[f % 2][:, 0:nv], sg[f % 2][:, 0:nv]
                        dve.wait_ge(up_done, i * KD + (f + 1))
                        dve.tensor_scalar(g, bank[b][:, 0:nv], b1c[1][:, f:f + 1], SWIGLU_LIMIT, ALU.add, ALU.min).then_inc(gate_ready, 1)
                        dve.tensor_scalar(u, bank[b + 1][:, 0:nv], b1c[1][:, KD + f:KD + f + 1], SWIGLU_LIMIT, ALU.add, ALU.min).then_inc(up_taken, 1)
                        dve.drain()
                        dve.tensor_scalar(u, u, -SWIGLU_LIMIT, 1.0, ALU.max, ALU.add)
                        dve.drain()
                        dve.wait_ge(sig_ready, i * KD + (f + 1))
                        dve.tensor_tensor(u, u, g, ALU.mult)
                        dve.drain()
                        dve.tensor_tensor(actT[:, f, 0:nv], u, s, ALU.mult).then_inc(act_ready, 1)
                by_slots(dve, n, body)

            def weigh_y(i):
                n = item(dve, 1, i)

                def tiles(nt):
                    for m in range(nt):
                        dve.wait_ge(y_turned, i * 2 * CT + (2 * m + 2))
                        dve.tensor_scalar(yrow[:, m, 512:1024], bank[7][:, :], gates_s[:, m:m + 1], None, ALU.mult).then_inc(yrow_dve, 1)
                    if nt < CT:
                        dve.sem_inc(yrow_dve, CT - nt)
                by_tiles(dve, n, tiles)

            def keep_slots(i, first=False):
                if not first:
                    dve.wait_ge(rows_added, 16 * CT * i)
                dve.tensor_copy(idxs, idxg)
                dve.tensor_copy(b1c[1], b1c[0])
                dve.tensor_copy(gates_s, gateg).then_inc(sslots_ready, 1)
                dve.drain()
            n_items = items(dve)
            slots(0)
            read_slots(0)
            turn_x(0)
            keep_slots(0, True)
            with dve.Fori(0, EXTRA) as i:
                with dve.If(i < n_items):
                    swiglu(i)
                    slots(i + 1)
                    read_slots(i + 1)
                    turn_x(i + 1)
                    weigh_y(i)
                    keep_slots(i + 1)
            dve.wait_ge(f_in[0], 16)
            dve.wait_ge(f_g, 16)
            for t in range(NT):
                dve.wait_ge(f_rms, t + 1)
                dve.reciprocal(rstd3[:, t:t + 1], rms3[:, t:t + 1])
                dve.drain()
                if t >= 2:
                    dve.wait_ge(f_out[t % 2], 16 * (t // 2))
                dve.scalar_tensor_tensor(out=yrow[:, t % 2, :], in0=xg[:, t % 2, :], scalar=rstd3[:, t:t + 1], in1=yrow[:, 2, :],
                                         op0=ALU.mult, op1=ALU.mult).then_inc(f_ready, 1)

        @block.tensor
        def _(pe):
            pe.wait_ge(route_in, 6 * 16)
            pe.wait_ge(order_in, 16)

            def turn_xn(t):
                pe.wait_ge(xn_ready, t + 1)
                for half in range(2):
                    if t >= 2:
                        pe.wait_ge(xnT_act if half == 0 else xnT_dve, t - 1)
                    for k in range(4):
                        ins = pe.transpose(bank[4 + 2 * (t % 2) + half][:, k * P:(k + 1) * P],
                                           xn[t % 2][:, (4 * half + k) * P:(4 * half + k + 1) * P], ident)
                    ins.then_inc(xn_turned, 1)

            def logits(t):
                pe.wait_ge(xnT_act, t + 1)
                pe.wait_ge(xnT_dve, t + 1)
                if t >= 2:
                    pe.wait_ge(logits_taken, t - 1)
                for k in range(KD):
                    ins = pe.matmul(bank[t % 2][:, 0:NEXP], xnT[t % 2][:, k, :], rw[:, k, :], start=(k == 0), stop=(k == KD - 1))
                ins.then_inc(logits_done, 1)
            for f in range(2 * KD):
                ins = pe.transpose(bank[3][:, f * NEXP:(f + 1) * NEXP], b1n[:, f * P:(f + 1) * P], ident[0:NEXP, 0:NEXP])
            ins.then_inc(b1_turned, 1)
            for t in range(NT):
                turn_xn(t)
                if t >= 1:
                    logits(t - 1)
            logits(NT - 1)
            pe.wait_ge(mask_ready, NT)
            for t in range(NT):
                for s in range(t + 1):
                    pe.matmul(bank[2][:, t * NEXP:(t + 1) * NEXP], ones_b if s < t else tri, maskb[:, s, 0:NEXP], start=(s == 0), stop=(s == t))
            for t in range(NT):
                pe.matmul(bank[2][:, 256:256 + NEXP], ones_b, maskb[:, t, 0:NEXP], start=(t == 0), stop=(t == NT - 1))
            for t in range(NT):
                ins = pe.matmul(bank[2][0:CANDS, 300:301], maskb[:, t, :], one_b, start=(t == 0), stop=(t == NT - 1))
            ins.then_inc(count_done, 1)
            for t in range(NT):
                ins = pe.transpose(bank[4 + t // 4][0:NEXP, (t % 4) * P:(t % 4 + 1) * P], gates[:, t, :], ident)
            ins.then_inc(gt_done, 1)
            pe.wait_ge(flag_ready, 1)
            pe.matmul(bank[0][0:CANDS, 0:1], cand_before, cand_flag, start=True, stop=True)
            pe.matmul(bank[0][:, 1:2], ones_f[0:CANDS, :], cand_flag, start=True, stop=True).then_inc(pos_done, 1)
            pe.wait_ge(cand_ready, 1)
            w = NLIST - NEXP
            for v in range(3):
                ins = pe.matmul(bank[1][:, v * w:(v + 1) * w], cand_v[0:CANDS, v, :], cand_hot[0:CANDS, :], start=True, stop=True)
            ins.then_inc(list_done, 1)
            pe.wait_ge(gt_taken, 1)
            for n in range(2 * NT):
                t, half = n // 2, n % 2
                if n >= 2:
                    pe.wait_ge(acc_ready, n - 1)
                pe.matmul(bank[6 + n % 2][:, :], gT[:, t * P:(t + 1) * P], b2n[:, half * 512:(half + 1) * 512],
                          start=True, stop=True).then_inc(b2_done, 1)

            def slots(i_next):
                pe.wait_ge(hot_ready, i_next + 1)
                for m in range(CT):
                    for t in range(NT):
                        ins = pe.matmul(bank[7][:, m * 6:(m + 1) * 6], onehot[:, t, m * P:(m + 1) * P], gcur[:, t, :],
                                        start=(t == 0), stop=(t == NT - 1))
                ins.then_inc(slots_done, 1)

            def turn_x(i_next):
                n = item(pe, 1, i_next)
                pe.wait_ge(rows_in, (i_next + 1) * 16 * CT)

                def tiles(nt):
                    for m in range(nt):
                        if m:
                            pe.wait_ge(xT_ready, i_next * 2 * CT + 2 * m)
                        for k in range(KD):
                            ins = pe.transpose(bank[6 + k // 4][:, (k % 4) * P:(k % 4 + 1) * P], xg[:, m, k * P:(k + 1) * P], ident)
                            if k % 4 == 3:
                                ins.then_inc(x_turned, 1)
                    if nt < CT:
                        pe.drain()
                        pe.sem_inc(x_turned, 2 * (CT - nt))
                by_tiles(pe, n, tiles)

            def up(i):
                n = item(pe, 1, i)
                pe.wait_ge(xT_ready, (i + 1) * 2 * CT)

                def body(nv):
                    for f in range(KD):
                        q, c = divmod(f * P, PC)
                        if c == 0:
                            pe.wait_ge(w1_in[q], (i + 1) * 32)
                        b = 2 * (f % 2)
                        if f >= 2:
                            pe.wait_ge(up_taken, i * KD + (f - 1))
                        for h in range(2):
                            for k in range(KD):
                                ins = pe.matmul(bank[b + h][:, 0:nv], w1r[:, q, k, h, c:c + P], xT[:, k, 0:nv], start=(k == 0), stop=(k == KD - 1))
                        ins.then_inc(up_done, 1)
                        if c + P == PC:
                            pe.drain()
                            pe.sem_inc(w1_used, 1)
                by_slots(pe, n, body)

            def down(i):
                n = item(pe, 1, i)

                def body(nv):
                    pe.wait_ge(act_ready, (i + 1) * KD)
                    for d in range(KD):
                        q, c = divmod(d * P, PC)
                        if c == 0:
                            pe.wait_ge(w2_in[q], (i + 1) * 16)
                        if d >= 2:
                            pe.wait_ge(down_taken, i * KD + (d - 1))
                        for k in range(KD):
                            ins = pe.matmul(bank[4 + d % 2][:, 0:nv], w2r[:, q, k, c:c + P], actT[:, k, 0:nv], start=(k == 0), stop=(k == KD - 1))
                        ins.then_inc(down_done, 1)
                        if c + P == PC:
                            pe.drain()
                            pe.sem_inc(w2_used, 1)
                by_slots(pe, n, body)

            def turn_y(i):
                n = item(pe, 1, i)
                pe.wait_ge(down_taken, (i + 1) * KD)
                pe.wait_ge(xT_ready, (i + 2) * 2 * CT)

                def tiles(nt):
                    for m in range(nt):
                        if m:
                            pe.wait_ge(yrow_act, i * CT + m)
                            pe.wait_ge(yrow_dve, i * CT + m)
                        for k in range(KD):
                            ins = pe.transpose(bank[6 + k // 4][:, (k % 4) * P:(k % 4 + 1) * P], yT[:, k, m * P:(m + 1) * P], ident)
                            if k % 4 == 3:
                                ins.then_inc(y_turned, 1)
                    if nt < CT:
                        pe.drain()
                        pe.sem_inc(y_turned, 2 * (CT - nt))
                by_tiles(pe, n, tiles)
            n_items = items(pe)
            pe.wait_ge(acc_ready, 2 * NT)
            slots(0)
            turn_x(0)
            with pe.Fori(0, EXTRA) as i:
                with pe.If(i < n_items):
                    up(i)
                    pe.wait_ge(sslots_ready, i + 1)
                    slots(i + 1)
                    down(i)
                    turn_x(i + 1)
                    turn_y(i)


_INS = ["x", "attn_norm_g", "w_in", "b_in", "swa_sinks", "diff_lambda_q1", "diff_lambda_k1", "diff_lambda_q2", "diff_lambda_k2",
        "diff_subln_g", "w_swa_out", "w_diff_out", "w_o", "ffn_norm_g", "router_w", "router_b", "w1", "b1", "w2", "b2", "final_norm_g"]


def kernel(**inputs):
    import concourse.bacc as bacc
    from concourse.bass_utils import run_bass_kernel_spmd

    nc = bacc.Bacc("TRN2", target_bir_lowering=False, num_devices=1)
    arrays, args = {}, {}
    for name in _INS:
        v = np.ascontiguousarray(inputs[name])
        arrays[f"in_{name}"] = v
        args[name] = nc.dram_tensor(f"in_{name}", v.shape, mybir.dt.from_np(v.dtype), kind="ExternalInput").ap()
    args["out"] = nc.dram_tensor("out_rows", (1, S, D), F32, kind="ExternalOutput").ap()
    program(nc, args)
    r = run_bass_kernel_spmd(nc, [arrays], core_ids=[0])
    return r.results[0]["out_rows"]
```

```python
import numpy as np
from contextlib import ExitStack

import concourse.bass as bass
from concourse import mybir

F32 = mybir.dt.float32
BF16 = mybir.dt.bfloat16
I32 = mybir.dt.int32
U32 = mybir.dt.uint32
ALU = mybir.AluOpType
ACT = mybir.ActivationFunctionType
AX = mybir.AxisListType

P = 128
D = 1024
S = 1024
NT = S // P
KD = D // P
HD = 64
NEXP, TOPK = 32, 4
FF = 1024
EPS = 1e-5
ATT_SCALE = HD ** -0.5
LAM_INIT = 0.8 - 0.6
NEG = -1.0e30
C_QA, C_KA, C_QB, C_KB, C_VB, C_GA, C_GB = 0, 512, 768, 1280, 1792, 2304, 3328
NCAT = C_GA
CHUNKS = [(C_QA, 512), (C_KA, 256), (C_QB, 512), (C_KB, 512), (C_VB, 512)]
TURNED_CHUNKS = 4
UNITS = [(kind, i, j) for i in range(NT) for j in range(4) for kind in ("swa", "diff")]
NU = len(UNITS)


def shape_constants():
    q, k = np.arange(P)[:, None], np.arange(P)[None, :]
    ident = np.eye(P, dtype=np.float32)
    causal = np.where(k <= q, 0.0, NEG).astype(np.float32)
    before = np.where(k > q, 0.0, NEG).astype(np.float32)
    pos = np.arange(S, dtype=np.float32)
    inv = np.float32(10000.0) ** (-np.arange(0, HD, 2, dtype=np.float32) / np.float32(HD))
    ang = (pos[:, None] * inv[None, :].astype(np.float32)).astype(np.float32)
    c, s = np.cos(ang).astype(np.float32), np.sin(ang).astype(np.float32)
    cos = np.concatenate([c, c], 1).reshape(NT, P, HD).transpose(1, 0, 2).reshape(P, NT * HD)
    sin = np.concatenate([-s, s], 1).reshape(NT, P, HD).transpose(1, 0, 2).reshape(P, NT * HD)
    return np.ascontiguousarray(np.concatenate([ident, before, causal], 1)), np.ascontiguousarray(np.concatenate([cos, sin], 1))


def units_before(kind, u):
    return sum(1 for x in UNITS[:u] if x[0] == kind)


def keys_of(unit):
    kind, i, _ = unit
    if kind == "diff":
        return list(range(i + 1))
    return [i - 1, i] if i else [0]


def program(nc, a):
    with ExitStack() as kept:
        tabs_s = kept.enter_context(nc.sbuf_tensor("tabs_s", [P, 3 * P], F32))
        reg_h = kept.enter_context(nc.sbuf_tensor("reg_h", [P, 8192], F32))
        reg_r = kept.enter_context(nc.sbuf_tensor("reg_r", [P, 3 * 8192], F32))
        x_back = kept.enter_context(nc.semaphore("x_back"))
        attention_half(nc, a, tabs_s, reg_h, reg_r, x_back)
        expert_half(nc, a, tabs_s, reg_h, reg_r, x_back)


def attention_half(nc, a, tabs_s, reg_h, reg_r, x_back):
    tabs, rope = shape_constants()
    tabs_d = nc.inline_tensor(tabs, name="masks_table").ap()
    rope_d = nc.inline_tensor(rope, name="rope_table").ap()
    ctx = ExitStack()
    with ctx:
        def sb(name, shape, dt=F32):
            return ctx.enter_context(nc.sbuf_tensor(name, shape, dt))

        def sem(name):
            return ctx.enter_context(nc.semaphore(name))

        pair = [ctx.enter_context(nc.psum_tensor(f"pair{i}", [P, 1024], F32)) for i in range(2)]
        bank = [pair[i // 2][:, 512 * (i % 2):512 * (i % 2 + 1)] for i in range(4)]
        bank += [ctx.enter_context(nc.psum_tensor(f"bank{i}", [P, 512], F32))[:, :] for i in range(4, 8)]

        ident, causal, band = tabs_s[:, 0:P], tabs_s[:, 2 * P:3 * P], tabs_s[:, P:3 * P]
        small = sb("small", [P, 256])
        eps_c = small[:, 0:1]
        ss1, rms1, rstd1 = small[:, 8:16], small[:, 16:24], small[:, 24:32]
        lam_s, lam_e, neg_lam = small[:, 32:34], small[:, 34:36], small[:, 36:37]
        mx, nm, lsum, rinv = small[:, 40:44], small[:, 44:48], small[:, 48:52], small[:, 52:60]
        sink_e, coef = small[:, 60:64], small[:, 64:66]
        ssb, rmsb, rstdb = small[:, 72:104], small[:, 104:136], small[:, 136:168]
        sinks, neg_sinks = small[:, 168:176], small[:, 176:184]
        gate_bias = small[:, 184:200]
        lamv = sb("lamv", [P, 4 * HD])
        subln = sb("subln", [P, 2 * HD])
        early = sb("early", [P, D + NCAT + 2 * NT * HD])
        g1_b = early[:, 0:D]
        bias_b = early[:, D:D + NCAT]
        cos_s = early[:, D + NCAT:D + NCAT + NT * HD].rearrange("p (t d) -> p t d", t=NT)
        sin_s = early[:, D + NCAT + NT * HD:].rearrange("p (t d) -> p t d", t=NT)
        reg_qa = sb("reg_qa", [P, 4096])
        reg_qb = sb("reg_qb", [P, 4096])
        reg_ka = sb("reg_ka", [P, 2048])
        reg_p = reg_r[:, 0:8192]
        reg_w = reg_r[:, 8192:16384]
        reg_kv = reg_r[:, 16384:]
        reg_g = sb("reg_g", [P, 2048])
        hT = reg_h[:, :].rearrange("p (k n) -> p k n", k=KD)
        x2 = reg_h[:, :].rearrange("p (t n) -> p t n", t=NT)
        qaT = reg_qa[:, :].rearrange("p (j n) -> p j n", j=4)
        qbT = reg_qb[:, :].rearrange("p (j n) -> p j n", j=4)
        kaT = reg_ka[:, 0:1024]
        va = reg_ka[:, 1024:2048].rearrange("p (t e) -> p t e", t=NT)
        kbT = reg_kv[:, 0:4096].rearrange("p (j n) -> p j n", j=4)
        vb = reg_kv[:, 4096:8192].rearrange("p (t e) -> p t e", t=NT)
        wo_s = reg_kv.rearrange("p (k n) -> p k n", k=KD)
        wch = [reg_w[:, i * 4096:(i + 1) * 4096] for i in range(2)]
        oan = reg_w[:, 0:4096].rearrange("p (t j e) -> p t j e", t=NT, j=4)
        obn = reg_w[:, 4096:8192].rearrange("p (t j e) -> p t j e", t=NT, j=4)
        mixT = reg_w.rearrange("p (k n) -> p k n", k=KD)
        xin = [reg_p[:, i * 1024:(i + 1) * 1024] for i in range(2)]
        hn = [reg_p[:, 2048 + i * 1024:2048 + (i + 1) * 1024] for i in range(2)]
        junk = reg_p[:, 4096:5120]
        biased = [reg_p[:, 5120 + i * 512:5120 + (i + 1) * 512] for i in range(2)]
        roped = [reg_p[:, 6144 + i * 512:6144 + (i + 1) * 512] for i in range(2)]
        rot = [reg_p[:, 7168 + i * 512:7168 + (i + 1) * 512] for i in range(2)]
        probs = [[reg_p[:, (2 * b + c) * 1024:(2 * b + c + 1) * 1024] for c in range(2)] for b in range(2)]
        pT = [reg_p[:, 4096 + b * 1024:4096 + (b + 1) * 1024] for b in range(2)]
        junk_o = reg_p[:, 6144:6144 + P]
        w_sd = reg_p.rearrange("p (a j n) -> p a j n", a=2, j=4)
        ring = [reg_ka[:, 0:1024], reg_ka[:, 1024:2048], reg_g[:, 0:1024], reg_g[:, 1024:2048]]
        sg = [[early[:, (2 * b + c) * 512:(2 * b + c + 1) * 512] for c in range(2)] for b in range(2)]

        first_in, rope_in, late_in = sem("first_in"), sem("rope_in"), sem("late_in")
        x_in = [sem("x_in0"), sem("x_in1")]
        rms_ready = sem("rms_ready")
        h_ready = sem("h_ready")
        h_turned = sem("h_turned")
        hT_act, hT_dve = sem("hT_act"), sem("hT_dve")
        w_in_s = [sem("w_in0"), sem("w_in1")]
        proj_done, proj_taken = sem("proj_done"), sem("proj_taken")
        rope_ready, rope_turned, qk_stored = sem("rope_ready"), sem("rope_turned"), sem("qk_stored")
        lam_dot, lam_exp = sem("lam_dot"), sem("lam_exp")
        score_ready, max_ready, exp_ready = sem("score_ready"), sem("max_ready"), sem("exp_ready")
        mix_ready, p_turned = sem("mix_ready"), sem("p_turned")
        pT_act, pT_dve = sem("pT_act"), sem("pT_dve")
        pv_ready, o_taken = sem("pv_ready"), sem("o_taken")
        subln_rms, subln_done = sem("subln_rms"), sem("subln_done")
        o_turned, oaT_ready, obT_ready = sem("o_turned"), sem("oaT_ready"), sem("obT_ready")
        wsd_in, wo_in = sem("wsd_in"), sem("wo_in")
        gw_in = [sem(f"gw_in{i}") for i in range(4)]
        gate_ready, gate_sig, y_ready, mix_done = sem("gate_ready"), sem("gate_sig"), sem("y_ready"), sem("mix_done")

        x_d = a["x"][0].rearrange("(t p) n -> t p n", p=P)
        w_in_d = a["w_in"][0].rearrange("(k p) n -> p k n", p=P)
        N_FIRST, N_ROPE, N_LATE = 2 * 16, 2 * 16, 10 * 16
        NPROJ = len(CHUNKS) * NT

        block = ctx.enter_context(nc.Block())

        @block.sync
        def _(sp):
            sp.dma_start(xin[0], x_d[0]).then_inc(x_in[0], 16)
            sp.dma_start(g1_b, a["attn_norm_g"][0].partition_broadcast(P)).then_inc(first_in, 16)
            sp.dma_start(tabs_s[:, :], tabs_d).then_inc(first_in, 16)
            sp.dma_start(xin[1], x_d[1]).then_inc(x_in[1], 16)

            def load_chunk(c):
                at, n = CHUNKS[c]
                if c >= 2:
                    sp.wait_ge(proj_done, NT * (c - 1))
                sp.dma_start(wch[c % 2][:, 0:8 * n].rearrange("p (k n) -> p k n", k=KD),
                             w_in_d[:, :, at:at + n]).then_inc(w_in_s[c % 2], 16)
            load_chunk(0)
            for t in range(2, NT):
                sp.wait_ge(h_ready, t - 1)
                sp.dma_start(xin[t % 2], x_d[t]).then_inc(x_in[t % 2], 16)
                if t == 3:
                    sp.dma_start(early[:, D + NCAT:], rope_d).then_inc(rope_in, 16)
                    sp.dma_start(bias_b, a["b_in"][0, 0:NCAT].partition_broadcast(P)).then_inc(rope_in, 16)
            load_chunk(1)
            for n, name in enumerate(("diff_lambda_q1", "diff_lambda_k1", "diff_lambda_q2", "diff_lambda_k2")):
                sp.dma_start(lamv[:, n * HD:(n + 1) * HD], a[name][0].partition_broadcast(P)).then_inc(late_in, 16)
            sp.dma_start(subln[:, :], a["diff_subln_g"][0].partition_broadcast(P)).then_inc(late_in, 16)
            sp.dma_start(sinks, a["swa_sinks"][0].partition_broadcast(P)).then_inc(late_in, 16)
            with nc.allow_non_contiguous_dma(reason="2048 gate biases, one for a partition"):
                for n in range(4):
                    sp.dma_start(gate_bias[:, 4 * n:4 * n + 4],
                                 a["b_in"][0, C_GA + 512 * n:C_GA + 512 * (n + 1)].rearrange("(k p) -> p k", p=P)).then_inc(late_in, 16)
            for c in range(2, len(CHUNKS)):
                load_chunk(c)
            w_ga_gb = [a["w_in"][0, :, at:at + D].rearrange("(k p) n -> p k n", p=P) for at in (C_GA, C_GB)]
            sp.wait_ge(pv_ready, NU)

            def load_gate(g):
                if g >= 4:
                    d, br = (g - 4) // 2, g % 2
                    sp.wait_ge(gate_ready, 4 * d + 3 + br)
                d, br = g // 2, g % 2
                sp.dma_start(ring[g % 4].rearrange("p (k n) -> p k n", k=KD),
                             w_ga_gb[br][:, :, d * P:(d + 1) * P]).then_inc(gw_in[g % 4], 16)
            for g in range(2):
                load_gate(g)
            w_swa = a["w_swa_out"][0].rearrange("(g j d) n -> g d j n", g=2, j=4)
            sp.wait_ge(o_taken, NU)
            for g in range(2):
                sp.dma_start(w_sd[64 * g:64 * g + 64, 0, :, :], w_swa[g]).then_inc(wsd_in, 16)
            sp.dma_start(w_sd[:, 1, :, :], a["w_diff_out"][0].rearrange("(j p) n -> p j n", p=P)).then_inc(wsd_in, 16)
            for g in range(2, 4):
                load_gate(g)
            sp.dma_start(wo_s, a["w_o"][0].rearrange("(k p) n -> p k n", p=P)).then_inc(wo_in, 16)
            for g in range(4, 2 * KD):
                load_gate(g)
            sp.wait_ge(gate_ready, 4 * KD)
            sp.dma_start(x2, a["x"][0].rearrange("(t p) n -> p t n", p=P)).then_inc(x_back, 16)

        @block.scalar
        def _(act):
            def norm_rms(t):
                act.wait_ge(x_in[t % 2], 16 * (t // 2 + 1))
                act.activation(junk, xin[t % 2], ACT.Square, accum_out=ss1[:, t:t + 1])
                act.drain()
                act.activation(rms1[:, t:t + 1], ss1[:, t:t + 1], ACT.Sqrt, bias=eps_c, scale=1.0 / D).then_inc(rms_ready, 1)

            def store_h(t):
                act.wait_ge(h_turned, 2 * t + 1)
                act.activation(hT[:, 0:4, t * P:(t + 1) * P], bank[4 + 2 * (t % 2)][:, :].rearrange("p (k n) -> p k n", k=4),
                               ACT.Copy).then_inc(hT_act, 1)
            act.wait_ge(lam_dot, 1)

            def store_qk(n):
                c, t = divmod(n, NT)
                act.wait_ge(rope_turned, n + 1)
                b = bank[2 + n % 2]
                blk = slice(t * P, (t + 1) * P)
                if c == 1:
                    act.activation(kaT[:, blk], b[:, 0:P], ACT.Copy).then_inc(qk_stored, 1)
                else:
                    dst = {0: qaT, 2: qbT, 3: kbT}[c]
                    act.activation(dst[:, :, blk], b[:, :].rearrange("p (j n) -> p j n", j=4), ACT.Copy).then_inc(qk_stored, 1)
            for t in range(NT + 1):
                if t < NT:
                    norm_rms(t)
                if t >= 1:
                    store_h(t - 1)
                if t >= 3:
                    store_qk(t - 3)
            for n in range(NT - 2, TURNED_CHUNKS * NT):
                store_qk(n)
            act.wait_ge(lam_dot, 3)
            act.activation(lam_e, lam_s, ACT.Exp).then_inc(lam_exp, 1)

            def exps(u):
                kind, i, j = UNITS[u]
                n = len(keys_of(UNITS[u])) * P
                for c in range(2):
                    act.wait_ge(max_ready, 2 * u + c + 1)
                    if c == 0 and u >= 2:
                        act.wait_ge(p_turned, 2 * (u - 1))
                    s = 2 * (u % 2) + c
                    act.activation(probs[u % 2][c][:, 0:n], pair[c][:, 0:n], ACT.Exp, bias=nm[:, s:s + 1],
                                   scale=ATT_SCALE, accum_out=lsum[:, s:s + 1]).then_inc(exp_ready, 1)
                    if kind == "swa":
                        head = j + 4 * c
                        act.activation(sink_e[:, s:s + 1], sinks[:, head:head + 1], ACT.Exp, bias=nm[:, s:s + 1]).then_inc(exp_ready, 1)

            def store_p(u):
                kind = UNITS[u][0]
                n = len(keys_of(UNITS[u])) * P * (2 if kind == "swa" else 1)
                act.wait_ge(p_turned, 2 * u + 1)
                if u >= 2:
                    act.wait_ge(pv_ready, u - 1)
                w = min(n, 512)
                act.activation(pT[u % 2][:, 0:w], bank[4][:, 0:w], ACT.Copy).then_inc(pT_act, 1)
            act.wait_ge(late_in, N_LATE)
            for u in range(NU + 1):
                if u < NU:
                    exps(u)
                if u >= 1:
                    store_p(u - 1)
            act.wait_ge(o_taken, NU)
            act.activation(rmsb, ssb, ACT.Sqrt, bias=eps_c, scale=1.0 / (2 * HD)).then_inc(subln_rms, 1)
            for i in range(NT):
                act.wait_ge(o_turned, 2 * i + 1)
                act.activation(qaT[:, :, i * P:(i + 1) * P], bank[2 * (i % 2)][:, :].rearrange("p (j n) -> p j n", j=4),
                               ACT.Copy).then_inc(oaT_ready, 1)
            for s in range(4 * KD):
                d, br = s // 4, s % 2
                act.wait_ge(gate_ready, s + 1)
                if s >= 4:
                    act.wait_ge(mix_done, s // 2 - 1)
                act.activation(sg[(s // 2) % 2][br], bank[br][:, :], ACT.Sigmoid,
                               bias=gate_bias[:, 8 * br + d:8 * br + d + 1]).then_inc(gate_sig, 1)

        @block.vector
        def _(dve):
            dve.memset(eps_c, EPS).then_inc(lam_dot, 1)

            def norm(t):
                dve.wait_ge(rms_ready, t + 1)
                dve.reciprocal(rstd1[:, t:t + 1], rms1[:, t:t + 1])
                dve.drain()
                if t >= 2:
                    dve.wait_ge(h_turned, 2 * (t - 1))
                dve.scalar_tensor_tensor(out=hn[t % 2], in0=xin[t % 2], scalar=rstd1[:, t:t + 1], in1=g1_b,
                                         op0=ALU.mult, op1=ALU.mult).then_inc(h_ready, 1)

            def store_h(t):
                dve.wait_ge(h_turned, 2 * t + 2)
                dve.tensor_copy(hT[:, 4:8, t * P:(t + 1) * P],
                                bank[5 + 2 * (t % 2)][:, :].rearrange("p (k n) -> p k n", k=4)).then_inc(hT_dve, 1)
            def bias_and_rope(n):
                c, t = divmod(n, NT)
                at, w = CHUNKS[c]
                if n == 0:
                    dve.wait_ge(rope_in, N_ROPE)
                dve.wait_ge(proj_done, n + 1)
                b = bank[n % 2]
                if c == 4:
                    dve.tensor_tensor(vb[:, t, :], b[:, :], bias_b[:, at:at + w], ALU.add).then_inc(proj_taken, 1)
                    return
                w = P if c == 1 else 512
                if c == 1:
                    dve.tensor_tensor(va[:, t, :], b[:, P:2 * P], bias_b[:, at + P:at + 2 * P], ALU.add)
                x = biased[n % 2]
                dve.tensor_tensor(x[:, 0:w], b[:, 0:w], bias_b[:, at:at + w], ALU.add).then_inc(proj_taken, 1)
                dve.drain()
                heads = w // HD
                xv = x[:, 0:w].rearrange("p (h s e) -> p h s e", h=heads, s=2)
                r = rot[n % 2]
                rv = r[:, 0:w].rearrange("p (h s e) -> p h s e", h=heads, s=2)
                sv = sin_s[:, t, :].rearrange("p (s e) -> p s e", s=2)
                for h in range(2):
                    dve.tensor_tensor(rv[:, :, h, :], xv[:, :, 1 - h, :],
                                      sv[:, h, :].unsqueeze(1).to_broadcast([P, heads, HD // 2]), ALU.mult)
                dve.drain()
                dve.tensor_tensor(x[:, 0:w].rearrange("p (h e) -> p h e", h=heads), x[:, 0:w].rearrange("p (h e) -> p h e", h=heads),
                                  cos_s[:, t, :].unsqueeze(1).to_broadcast([P, heads, HD]), ALU.mult)
                dve.drain()
                if n >= 2:
                    dve.wait_ge(rope_turned, n - 1)
                o = roped[n % 2]
                if c == 0:
                    dve.tensor_tensor(o.rearrange("p (j g e) -> p g j e", j=4, g=2), x.rearrange("p (g j e) -> p g j e", g=2, j=4),
                                      r.rearrange("p (g j e) -> p g j e", g=2, j=4), ALU.add).then_inc(rope_ready, 1)
                else:
                    dve.tensor_tensor(o[:, 0:w], x[:, 0:w], r[:, 0:w], ALU.add).then_inc(rope_ready, 1)
            dve.wait_ge(first_in, N_FIRST)
            for t in range(NT + 1):
                if t < NT:
                    norm(t)
                if t >= 1:
                    store_h(t - 1)
                if t >= 2:
                    bias_and_rope(t - 2)
            for n in range(NT - 1, NPROJ):
                bias_and_rope(n)
            dve.wait_ge(late_in, N_LATE)
            for n in range(2):
                dve.tensor_tensor_reduce(junk_o[:, n * HD:(n + 1) * HD], lamv[:, 2 * n * HD:(2 * n + 1) * HD],
                                         lamv[:, (2 * n + 1) * HD:(2 * n + 2) * HD], 1.0, 0.0, ALU.mult, ALU.add,
                                         lam_s[:, n:n + 1]).then_inc(lam_dot, 1)
            dve.tensor_scalar(neg_sinks, sinks, -1.0, None, ALU.mult)
            dve.tensor_scalar(subln[:, :], subln[:, :], 1.0 - LAM_INIT, None, ALU.mult)
            dve.wait_ge(lam_exp, 1)
            dve.tensor_tensor(neg_lam, lam_e[:, 1:2], lam_e[:, 0:1], ALU.subtract)
            dve.drain()
            dve.tensor_scalar(neg_lam, neg_lam, -LAM_INIT, None, ALU.add)

            def maxima(u):
                kind, i, j = UNITS[u]
                keys = keys_of(UNITS[u])
                for c in range(2):
                    s = 2 * (u % 2) + c
                    dve.wait_ge(score_ready, 2 * u + c + 1)
                    n = len(keys) * P
                    masked = 2 * P if kind == "swa" and i else P
                    v = pair[c][:, n - masked:n]
                    dve.tensor_tensor_reduce(v, v, band if masked > P else causal, 1.0, NEG, ALU.add, ALU.max, mx[:, s:s + 1])
                    if n > masked:
                        dve.tensor_reduce(coef[:, c:c + 1], pair[c][:, 0:n - masked], AX.X, ALU.max)
                    dve.drain()
                    if kind == "swa":
                        head = j + 4 * c
                        dve.tensor_scalar(nm[:, s:s + 1], mx[:, s:s + 1], -ATT_SCALE, neg_sinks[:, head:head + 1],
                                          ALU.mult, ALU.min).then_inc(max_ready, 1)
                    elif n > masked:
                        dve.tensor_scalar(nm[:, s:s + 1], mx[:, s:s + 1], coef[:, c:c + 1], -ATT_SCALE, ALU.max, ALU.mult).then_inc(max_ready, 1)
                    else:
                        dve.tensor_scalar(nm[:, s:s + 1], mx[:, s:s + 1], -ATT_SCALE, None, ALU.mult).then_inc(max_ready, 1)

            def exp_count(u):
                return 2 * u + 2 * units_before("swa", u)

            def mix(u):
                kind, i, j = UNITS[u]
                n = len(keys_of(UNITS[u])) * P
                dve.wait_ge(exp_ready, exp_count(u + 1))
                s = 2 * (u % 2)
                r = rinv[:, 2 * (u % 4):2 * (u % 4) + 2]
                if kind == "swa":
                    dve.tensor_tensor(lsum[:, s:s + 2], lsum[:, s:s + 2], sink_e[:, s:s + 2], ALU.add)
                    dve.drain()
                    dve.reciprocal(r, lsum[:, s:s + 2]).then_inc(mix_ready, 1)
                    return
                dve.reciprocal(r, lsum[:, s:s + 2])
                dve.drain()
                dve.scalar_tensor_tensor(out=coef[:, 0:1], in0=lsum[:, s:s + 1], scalar=neg_lam, in1=r[:, 1:2],
                                         op0=ALU.mult, op1=ALU.mult)
                dve.drain()
                pr = probs[u % 2]
                dve.scalar_tensor_tensor(out=pr[0][:, 0:n], in0=pr[1][:, 0:n], scalar=coef[:, 0:1], in1=pr[0][:, 0:n],
                                         op0=ALU.mult, op1=ALU.add).then_inc(mix_ready, 1)

            def store_p(u):
                kind, i, j = UNITS[u]
                n = len(keys_of(UNITS[u])) * P
                if kind == "swa" or n <= 512:
                    return
                dve.wait_ge(p_turned, 2 * u + 2)
                if u >= 2:
                    dve.wait_ge(pv_ready, u - 1)
                dve.tensor_copy(pT[u % 2][:, 512:n], bank[5][:, 0:n - 512]).then_inc(pT_dve, 1)

            def finish(u):
                kind, i, j = UNITS[u]
                dve.wait_ge(pv_ready, u + 1)
                r = rinv[:, 2 * (u % 4):2 * (u % 4) + 2]
                o = bank[6 + u % 2]
                if kind == "swa":
                    for c in range(2):
                        ins = dve.tensor_scalar(oan[:, i, j, c * HD:(c + 1) * HD], o[:, c * HD:(c + 1) * HD], r[:, c:c + 1], None, ALU.mult)
                    ins.then_inc(o_taken, 1)
                else:
                    dve.tensor_scalar(obn[:, i, j, :], o[:, 0:P], r[:, 0:1], None, ALU.mult)
                    dve.drain()
                    dve.tensor_tensor_reduce(junk_o, obn[:, i, j, :], obn[:, i, j, :], 1.0, 0.0, ALU.mult, ALU.add,
                                             ssb[:, 4 * i + j:4 * i + j + 1]).then_inc(o_taken, 1)
            for u in range(NU + 2):
                if 1 <= u <= NU:
                    mix(u - 1)
                if u < NU:
                    maxima(u)
                if 1 <= u <= NU:
                    store_p(u - 1)
                if u >= 2:
                    finish(u - 2)
            dve.wait_ge(subln_rms, 1)
            dve.reciprocal(rstdb, rmsb)
            dve.drain()
            for i in range(NT):
                o = obn[:, i, :, :]
                dve.tensor_tensor(o, o, rstdb[:, 4 * i:4 * i + 4].unsqueeze(2).to_broadcast([P, 4, P]), ALU.mult)
                dve.drain()
                dve.tensor_tensor(o, o, subln[:, :].unsqueeze(1).to_broadcast([P, 4, P]), ALU.mult).then_inc(subln_done, 1)
                if i >= 1:
                    dve.wait_ge(o_turned, 2 * i)
                    dve.tensor_copy(qbT[:, :, (i - 1) * P:i * P],
                                    bank[1 + 2 * ((i - 1) % 2)][:, :].rearrange("p (j n) -> p j n", j=4)).then_inc(obT_ready, 1)
            i = NT
            dve.wait_ge(o_turned, 2 * i)
            dve.tensor_copy(qbT[:, :, (i - 1) * P:i * P],
                            bank[1 + 2 * ((i - 1) % 2)][:, :].rearrange("p (j n) -> p j n", j=4)).then_inc(obT_ready, 1)
            for m in range(2 * KD):
                d, half = m // 2, m % 2
                for br in range(2):
                    dve.wait_ge(gate_sig, 2 * m + br + 1)
                    dve.wait_ge(y_ready, 2 * m + br + 1)
                    g = sg[m % 2][br]
                    ins = dve.tensor_tensor(g, g, bank[2 + br + 2 * (m % 2)], ALU.mult)
                dve.drain()
                dve.tensor_tensor(mixT[:, d, half * 512:(half + 1) * 512], sg[m % 2][0], sg[m % 2][1], ALU.add).then_inc(mix_done, 1)

        @block.tensor
        def _(pe):
            pe.wait_ge(first_in, N_FIRST)

            def turn_h(t):
                pe.wait_ge(h_ready, t + 1)
                for half in range(2):
                    if t >= 2:
                        pe.wait_ge(hT_act if half == 0 else hT_dve, t - 1)
                    for k in range(4):
                        ins = pe.transpose(bank[4 + 2 * (t % 2) + half][:, k * P:(k + 1) * P],
                                           hn[t % 2][:, (4 * half + k) * P:(4 * half + k + 1) * P], ident)
                    ins.then_inc(h_turned, 1)

            def project(n):
                c, t = divmod(n, NT)
                w = CHUNKS[c][1]
                if t == 0:
                    pe.wait_ge(w_in_s[c % 2], 16 * (c // 2 + 1))
                if n >= 2:
                    pe.wait_ge(proj_taken, n - 1)
                if c == 0:
                    pe.wait_ge(hT_act, t + 1)
                    pe.wait_ge(hT_dve, t + 1)
                wv = wch[c % 2][:, 0:8 * w].rearrange("p (k n) -> p k n", k=KD)
                for k in range(KD):
                    ins = pe.matmul(bank[n % 2][:, 0:w], hT[:, k, t * P:(t + 1) * P], wv[:, k, :], start=(k == 0), stop=(k == KD - 1))
                ins.then_inc(proj_done, 1)

            def turn_rope(n):
                c, t = divmod(n, NT)
                if c >= TURNED_CHUNKS:
                    return
                pe.wait_ge(rope_ready, n + 1)
                if n >= 2:
                    pe.wait_ge(qk_stored, n - 1)
                for j in range(1 if c == 1 else 4):
                    ins = pe.transpose(bank[2 + n % 2][:, j * P:(j + 1) * P], roped[n % 2][:, j * P:(j + 1) * P], ident)
                ins.then_inc(rope_turned, 1)
            for t in range(NT):
                turn_h(t)
                if t >= 1:
                    project(t - 1)
                if t >= 2:
                    turn_rope(t - 2)
            for n in range(NT - 1, NPROJ):
                project(n)
                turn_rope(n - 1)
            turn_rope(NPROJ - 1)

            def scores(u):
                kind, i, j = UNITS[u]
                keys = keys_of(UNITS[u])
                k0, n = keys[0] * P, len(keys) * P
                for c in range(2):
                    if u >= 1:
                        sinks_too = UNITS[u - 1][0] == "swa"
                        pe.wait_ge(exp_ready, 2 * (u - 1) + 2 * units_before("swa", u - 1) + (1 if c == 0 else 3 if sinks_too else 2))
                    q = (qaT if kind == "swa" else qbT)[64 * c:64 * c + 64, j, i * P:(i + 1) * P]
                    kk = (kaT[64 * c:64 * c + 64, :] if kind == "swa" else kbT[64 * c:64 * c + 64, j, :])
                    for h in range(0, n, 512):
                        w = min(512, n - h)
                        ins = pe.matmul(pair[c][:, h:h + w], q, kk[:, k0 + h:k0 + h + w], start=True, stop=True)
                    ins.then_inc(score_ready, 1)

            def turn_p(u):
                kind, i, j = UNITS[u]
                n = len(keys_of(UNITS[u]))
                pe.wait_ge(mix_ready, u + 1)
                if u >= 1:
                    pe.wait_ge(pT_act, u)
                    done = sum(1 for x in UNITS[:u] if x[0] == "diff" and len(keys_of(x)) > 4)
                    if done:
                        pe.wait_ge(pT_dve, done)
                tiles = [(c, m) for c in range(2) for m in range(n)] if kind == "swa" else [(0, m) for m in range(n)]
                for at, (c, m) in enumerate(tiles):
                    ins = pe.transpose(bank[4 + at // 4][:, (at % 4) * P:(at % 4 + 1) * P],
                                       probs[u % 2][c][:, m * P:(m + 1) * P], ident)
                    if at == len(tiles) - 1:
                        ins.then_inc(p_turned, 1 if at > 3 else 2)
                    elif at == 3:
                        ins.then_inc(p_turned, 1)

            def product(u):
                kind, i, j = UNITS[u]
                keys = keys_of(UNITS[u])
                pe.wait_ge(pT_act, u + 1)
                done = sum(1 for x in UNITS[:u + 1] if x[0] == "diff" and len(keys_of(x)) > 4)
                if done:
                    pe.wait_ge(pT_dve, done)
                if u >= 2:
                    pe.wait_ge(o_taken, u - 1)
                o = bank[6 + u % 2]
                if kind == "swa":
                    for c in range(2):
                        for m, kt in enumerate(keys):
                            at = c * len(keys) + m
                            ins = pe.matmul(o[:, c * HD:(c + 1) * HD], pT[u % 2][:, at * P:(at + 1) * P],
                                            va[:, kt, c * HD:(c + 1) * HD], start=(m == 0), stop=(m == len(keys) - 1))
                else:
                    for m, kt in enumerate(keys):
                        ins = pe.matmul(o[:, 0:P], pT[u % 2][:, m * P:(m + 1) * P], vb[:, kt, j * P:(j + 1) * P],
                                        start=(m == 0), stop=(m == len(keys) - 1))
                ins.then_inc(pv_ready, 1)
            pe.wait_ge(qk_stored, TURNED_CHUNKS * NT)
            pe.wait_ge(proj_taken, NPROJ)
            for u in range(NU + 2):
                if u < NU:
                    scores(u)
                if u >= 2:
                    product(u - 2)
                if 1 <= u <= NU:
                    turn_p(u - 1)
            for i in range(NT):
                if i >= 2:
                    pe.wait_ge(oaT_ready, i - 1)
                else:
                    pe.wait_ge(o_taken, NU)
                for j in range(4):
                    ins = pe.transpose(bank[2 * (i % 2)][:, j * P:(j + 1) * P], oan[:, i, j, :], ident)
                ins.then_inc(o_turned, 1)
                pe.wait_ge(subln_done, i + 1)
                if i >= 2:
                    pe.wait_ge(obT_ready, i - 1)
                for j in range(4):
                    ins = pe.transpose(bank[1 + 2 * (i % 2)][:, j * P:(j + 1) * P], obn[:, i, j, :], ident)
                ins.then_inc(o_turned, 1)
            pe.wait_ge(wsd_in, 48)
            pe.wait_ge(oaT_ready, NT)
            pe.wait_ge(obT_ready, NT)
            for m in range(2 * KD):
                d, half = m // 2, m % 2
                tok = slice(half * 512, (half + 1) * 512)
                for br in range(2):
                    g = 2 * d + br
                    if half == 0:
                        pe.wait_ge(gw_in[g % 4], 16 * (g // 4 + 1))
                    if m >= 1:
                        pe.wait_ge(gate_sig, 2 * m + br - 1)
                    wv = ring[g % 4].rearrange("p (k n) -> p k n", k=KD)
                    for k in range(KD):
                        ins = pe.matmul(bank[br][:, :], wv[:, k, :], hT[:, k, tok], start=(k == 0), stop=(k == KD - 1))
                    ins.then_inc(gate_ready, 1)
                for br in range(2):
                    if m >= 2:
                        pe.wait_ge(mix_done, m - 1)
                    oT = (qaT, qbT)[br]
                    for j in range(4):
                        ins = pe.matmul(bank[2 + br + 2 * (m % 2)], w_sd[:, br, j, d * P:(d + 1) * P], oT[:, j, tok],
                                        start=(j == 0), stop=(j == 3))
                    ins.then_inc(y_ready, 1)
            pe.wait_ge(wo_in, 16)


CAP = 384
CT = CAP // P
VARIANTS = [96] + list(range(128, CAP + 1, 16))
MAX_ITEMS = NEXP + (S * TOPK) // (CAP + 1)
NLIST = 48
CANDS = 2 * NEXP
ROWS = S + CAP
PIECES = 4
PC = FF // PIECES
SWIGLU_LIMIT, SWIGLU_ALPHA = 7.0, 1.702


def expert_constants():
    p = np.arange(P)
    f = np.zeros((P, 640), np.float32)
    f[:, 0:CAP] = np.arange(CAP)[None, :]
    f[:, 384:387] = S + p[:, None] + P * np.arange(CT)[None, :]
    f[:CANDS, 387] = CAP * (1 + p[:CANDS] // NEXP)
    f[:CANDS, 388] = p[:CANDS] % NEXP
    f[:, 389] = 1.0
    f[:CANDS, 400:464] = (p[:CANDS, None] < p[None, :CANDS])
    f[:, 464:592] = 1.0
    b = np.zeros((P, 256 + 8 * 6 + 1), np.float32)
    b[:, 0:128] = (p[:, None] < p[None, :])
    b[:, 128:256] = 1.0
    g = b[:, 256:304].reshape(P, 8, 6)
    g[:, :, 0] = np.arange(8)[None, :]
    g[:, :, 1] = p[:, None]
    g[:, :, 2] = 1.0
    b[:, 304] = 1.0
    return f, b


def expert_half(nc, a, tabs_s, reg_h, reg_r, x_back):
    fc, bc = expert_constants()
    fc_d = nc.inline_tensor(fc, name="slot_table").ap()
    bc_d = nc.inline_tensor(bc, name="order_table").ap()
    ident = tabs_s[:, 0:P]
    xn_d = nc.dram_tensor("xn_rows", [ROWS, D], F32, kind="Internal").ap()
    acc_d = nc.dram_tensor("acc_rows", [ROWS, D], F32, kind="Internal").ap()
    with ExitStack() as ctx:
        def sb(name, shape, dt=F32):
            return ctx.enter_context(nc.sbuf_tensor(name, shape, dt))

        def sem(name):
            return ctx.enter_context(nc.semaphore(name))

        bank = [ctx.enter_context(nc.psum_tensor(f"xbank{i}", [P, 512], F32)) for i in range(8)]
        x2 = reg_h[:, :].rearrange("p (t n) -> p t n", t=NT)
        w1r = reg_r[:, 0:16384].rearrange("p (q k h c) -> p q k h c", q=PIECES, k=KD, h=2)
        w2r = reg_r[:, 16384:].rearrange("p (q k c) -> p q k c", q=PIECES, k=KD)
        mixT = reg_r[:, 8192:16384].rearrange("p (k n) -> p k n", k=KD)
        wo_s = reg_r[:, 16384:].rearrange("p (k n) -> p k n", k=KD)
        xg = sb("xg", [P, CT, D])
        xT = sb("xT", [P, KD, CAP])
        actT = sb("actT", [P, KD, CAP])
        yT = sb("yT", [P, KD, CAP])
        yrow = sb("yrow", [P, CT, D])
        b1T = sb("b1T", [P, NEXP, 2 * KD])
        rankm = sb("rankm", [P, NEXP, NT])
        gparts = sb("gparts", [P, NEXP, NT, 3], BF16)
        fcs = sb("fcs", [P, 640])
        bcs = sb("bcs", [P, 305], BF16)
        lists = sb("lists", [P, 3, NLIST])
        listi = sb("listi", [P, 3, NLIST], I32)
        nitem = sb("nitem", [P, 1], I32)
        sm = sb("sm", [P, 512])
        onehot = sb("onehot", [P, NT, CAP], BF16)
        gl, ul, sg = ([reg_h[:, (2 * v + n) * CAP:(2 * v + n + 1) * CAP] for n in range(2)] for v in range(3))
        xgf, xTf, actf, yTf, yrf = (v[:, :, :].rearrange("p a b -> p (a b)") for v in (xg, xT, actT, yT, yrow))
        xn = [xgf[:, 0:D], xgf[:, D:2 * D]]
        g2_b = xgf[:, 2 * D:3 * D]
        xnT = [xTf[:, n * D:(n + 1) * D].rearrange("p (k s) -> p k s", k=KD) for n in range(2)]
        junk = xTf[:, 2 * D:3 * D]
        b1n = actf[0:NEXP, 0:2 * FF]
        rw = actf[:, 2 * FF:2 * FF + 256].rearrange("p (k e) -> p k e", k=KD)
        rb_b = actf[:, 2 * FF + 256:2 * FF + 288]
        b2n = yTf[0:NEXP, 0:D]
        gT = yTf[0:NEXP, D:2 * D]
        zero = yTf[:, 2 * D:3 * D]
        lg = yrf[:, 0:256].rearrange("p (t e) -> p t e", t=NT)
        gates = yrf[:, 256:512].rearrange("p (t e) -> p t e", t=NT)
        hot = yrf[:, 512:640].rearrange("p (k e) -> p k e", k=TOPK)
        maskf = yrf[:, 640:896].rearrange("p (t e) -> p t e", t=NT)
        maskb = yrf[:, 896:1152].bitcast(BF16).rearrange("p (t e) -> p t e", t=NT)
        gres = yrf[:, 1152:1408].rearrange("p (e t) -> p e t", t=NT)
        gres2 = yrf[:, 1408:1664].rearrange("p (e t) -> p e t", t=NT)
        cand_v = yrf[:, 1664:1664 + 3 * P].rearrange("p (v n) -> p v n", v=3)
        cand_hot = yrf[:, 2048:2048 + NLIST - NEXP]
        iota_e = fcs[:, 0:NEXP]
        iota_s = fcs[:, 0:CAP]
        unused_row = fcs[:, 384:387]
        cand_first, cand_exp = fcs[0:CANDS, 387:388], fcs[0:CANDS, 388:389]
        cand_before = fcs[0:CANDS, 400:464]
        ones_f = fcs[:, 464:592]
        tri, ones_b = bcs[:, 0:P], bcs[:, P:2 * P]
        gcur = bcs[:, 256:304].rearrange("p (t v) -> p t v", t=NT)
        one_b = bcs[:, 304:305]
        eps_c = sm[:, 0:1]
        ss2, rms2, rstd2 = sm[:, 8:16], sm[:, 16:24], sm[:, 24:32]
        top = sm[:, 32:96].rearrange("p (t k) -> p t k", t=NT)
        topi = sm[:, 96:160].bitcast(U32).rearrange("p (t k) -> p t k", t=NT)
        topf = sm[:, 160:192].rearrange("p (t k) -> p t k", t=NT)
        ex = sm[:, 192:224].rearrange("p (t k) -> p t k", t=NT)
        ntop, exs, rexs = sm[:, 224:232], sm[:, 232:240], sm[:, 240:248]
        cand_n, cand_flag, cand_pos = sm[0:CANDS, 248:249], sm[0:CANDS, 249:250], sm[0:CANDS, 250:251]
        rk, rk0, basec = sm[:, 256:264], sm[:, 264:272], sm[:, 272:273]
        b1c = sm[:, 280:296]
        idxa, gatea = sm[:, 344:347].bitcast(I32), sm[:, 348:351]
        idxf, padf = sm[:, 320:323], sm[:, 324:327]
        idxg, gateg = sm[:, 328:331].bitcast(I32), sm[:, 332:335]
        idxs, gates_s = sm[:, 336:339].bitcast(I32), sm[:, 340:343]
        ss3, rms3, rstd3 = sm[:, 352:360], sm[:, 360:368], sm[:, 368:376]
        spare = sm[0:1, 384:400]

        route_in, xn_out, acc_out, zero_out = sem("route_in"), [sem("xn_out0"), sem("xn_out1")], sem("acc_out"), sem("zero_out")
        consts_ready, order_in = sem("consts_ready"), sem("order_in")
        rms2_ready, xn_ready, xn_turned, xnT_act, xnT_dve = (sem(n) for n in ("rms2_ready", "xn_ready", "xn_turned", "xnT_act", "xnT_dve"))
        logits_done, logits_taken, top_ready, ex_ready, mask_ready = (sem(n) for n in ("logits_done", "logits_taken", "top_ready", "ex_ready", "mask_ready"))
        count_done, flag_ready, pos_done, cand_ready, list_done, list_ready = (
            sem(n) for n in ("count_done", "flag_ready", "pos_done", "cand_ready", "list_done", "list_ready"))
        gt_done, gt_taken, b2_done, acc_ready = (sem(n) for n in ("gt_done", "gt_taken", "b2_done", "acc_ready"))
        b1_turned, b1_taken = sem("b1_turned"), sem("b1_taken")
        w1_in = [sem(f"w1_in{q}") for q in range(PIECES)]
        w2_in = [sem(f"w2_in{q}") for q in range(PIECES)]
        o_proj, x2_done = sem("o_proj"), sem("x2_done")
        hot_ready, slots_done, slots_ready = sem("hot_ready"), sem("slots_done"), sem("slots_ready")
        rows_in, waits_taken = sem("rows_in"), sem("waits_taken")
        x_turned, xT_act, xT_dve = sem("x_turned"), sem("xT_act"), sem("xT_dve")
        up_done, up_taken, gate_ready, sig_ready, act_ready = (sem(n) for n in ("up_done", "up_taken", "gate_min", "sig_ready", "act_ready"))
        down_done, down_taken = sem("down_done"), sem("down_taken")
        y_turned, yrow_act, yrow_dve, sslots_ready, rows_added = (
            sem(n) for n in ("y_turned", "yrow_act", "yrow_dve", "sslots_ready", "rows_added"))
        f_g = sem("f_g")
        f_in, f_rms, f_ready, f_out = [sem(f"f_in{t}") for t in range(NT)], sem("f_rms"), sem("f_ready"), sem("f_out")
        fin = [v[:, n * D:(n + 1) * D] for v in (xgf, xTf, actf) for n in range(3)][:NT]
        fin_g, fin_junk = yTf[:, 0:D], yrf[:, 0:D]

        def by_slots(eng, count, body):
            def choose(vs):
                if len(vs) == 1:
                    body(vs[0])
                    return
                half = (len(vs) + 1) // 2
                with eng.If(count <= vs[half - 1]):
                    choose(vs[:half])
                with eng.Else():
                    choose(vs[half:])
            choose(VARIANTS)

        def by_tiles(eng, count, body):
            with eng.If(count <= P):
                body(1)
            with eng.Else():
                with eng.If(count <= 2 * P):
                    body(2)
                with eng.Else():
                    body(3)

        def item(eng, what, i):
            return eng.value_load(listi[0:1, what, bass.ds(i, 1)], min_val=0, max_val=(NEXP - 1, CAP)[what])

        def items(eng):
            eng.wait_ge(list_ready, 1)
            return eng.value_load(nitem[0:1, 0:1], min_val=NEXP, max_val=MAX_ITEMS)

        w1_d = a["w1"][0].rearrange("e (k p) (h q c) -> e q p k h c", p=P, h=2, q=PIECES)
        w2_d = a["w2"][0].rearrange("e (k p) (q c) -> e q p k c", p=P, q=PIECES)
        fin_d = a["out"][0].rearrange("(t p) n -> t p n", p=P)

        block = ctx.enter_context(nc.Block())

        @block.sync
        def _(sp):
            sp.dma_start(fcs[:, :], fc_d).then_inc(route_in, 16)
            sp.dma_start(g2_b, a["ffn_norm_g"][0].partition_broadcast(P)).then_inc(route_in, 16)
            sp.dma_start(rw, a["router_w"][0].rearrange("(k p) e -> p k e", p=P)).then_inc(route_in, 16)
            sp.dma_start(rb_b, a["router_b"][0].partition_broadcast(P)).then_inc(route_in, 16)
            sp.dma_start(b1n, a["b1"][0]).then_inc(route_in, 16)
            sp.dma_start(b2n, a["b2"][0]).then_inc(route_in, 16)
            sp.wait_ge(consts_ready, 2)
            for m in range(CT):
                sp.dma_start(xn_d[S + m * P:S + (m + 1) * P, :], zero).then_inc(zero_out, 16)
                sp.dma_start(acc_d[S + m * P:S + (m + 1) * P, :], zero).then_inc(zero_out, 16)
            def first_piece(q):
                for half in range(2):
                    sp.dma_start(w1r[:, q, :, half, :], w1_d[0, q, :, :, half, :]).then_inc(w1_in[q], 16)
            for q in range(PIECES // 2):
                first_piece(q)
            for t in range(NT):
                sp.wait_ge(xn_ready, t + 1)
                sp.dma_start(xn_d[t * P:(t + 1) * P, :], xn[t % 2]).then_inc(xn_out[t % 2], 16)
            sp.wait_ge(o_proj, 2 * NT)
            for q in range(PIECES // 2, PIECES):
                first_piece(q)
            for q in range(PIECES):
                sp.dma_start(w2r[:, q, :, :], w2_d[0, q]).then_inc(w2_in[q], 16)
            for t in range(NT):
                sp.wait_ge(acc_ready, 2 * (t + 1))
                sp.dma_start(acc_d[t * P:(t + 1) * P, :], x2[:, t, :]).then_inc(acc_out, 16)
            n_items = items(sp)
            with sp.Fori(0, MAX_ITEMS - 1) as i:
                with sp.If(i + 1 < n_items):
                    e = item(sp, 0, i + 1)
                    for q in range(PIECES):
                        sp.wait_ge(up_done, i * KD + (q + 1) * (KD // PIECES))
                        for half in range(2):
                            sp.dma_start(w1r[:, q, :, half, :],
                                         w1_d[bass.ds(e, 1), q, :, :, half, :].rearrange("o p k c -> (o p) k c")).then_inc(w1_in[q], 16)
                    for q in range(PIECES):
                        sp.wait_ge(down_done, i * KD + (q + 1) * (KD // PIECES))
                        sp.dma_start(w2r[:, q, :, :], w2_d[bass.ds(e, 1), q].rearrange("o p k c -> (o p) k c")).then_inc(w2_in[q], 16)
            sp.wait_ge(rows_added, n_items * (16 * CT) + 16)
            sp.dma_start(fin_g, a["final_norm_g"].partition_broadcast(P)).then_inc(f_g, 16)
            for t in range(NT):
                sp.dma_start(fin[t], acc_d[t * P:(t + 1) * P, :]).then_inc(f_in[t], 16)
            for t in range(NT):
                sp.wait_ge(f_ready, t + 1)
                sp.dma_start(fin_d[t], fin[t]).then_inc(f_out, 16)
            sp.wait_ge(f_out, 16 * NT)

        @block.gpsimd
        def _(pool):
            pool.dma_start(bcs[:, :], bc_d).then_inc(order_in, 16)

            def take_waits(before):
                pool.wait_ge(waits_taken, before)
                pool.tensor_tensor(spare[:, 8:9], fcs[0:1, 0:1], fcs[0:1, 1:2], ALU.add).then_inc(waits_taken, 1)
            pool.memset(spare[:, 8:9], 0.0).then_inc(waits_taken, 1)

            def gather(i_next, n):

                def rows(tiles):
                    pool.wait_ge(slots_ready, i_next + 1)
                    if not (isinstance(i_next, int) and i_next == 0):
                        pool.wait_ge(x_turned, CT * 2 * i_next)
                        take_waits(2 * i_next - 2 if isinstance(i_next, bass.RuntimeValue) else 1)
                    for m in range(tiles):
                        pool.indirect_dma_start(out=xg[:, m, :], out_offset=None, in_=xn_d,
                                                in_offset=bass.IndirectOffsetOnAxis(ap=idxg[:, m:m + 1].bitcast(U32), axis=0)).then_inc(rows_in, 16)
                    for m in range(tiles, CT):
                        pool.dma_start(spare[:, m:m + 1], fcs[0:1, m:m + 1]).then_inc(rows_in, 16)
                by_tiles(pool, n, rows)

            def scatter(i, n):

                def rows(tiles):
                    pool.wait_ge(sslots_ready, i + 1)
                    pool.wait_ge(yrow_act, CT * (i + 1) + 1)
                    pool.wait_ge(yrow_dve, CT * (i + 1) + 1)
                    take_waits(2 * i + 3)
                    for m in range(tiles):
                        pool.indirect_dma_start(out=acc_d, out_offset=bass.IndirectOffsetOnAxis(ap=idxs[:, m:m + 1].bitcast(U32), axis=0),
                                                in_=yrow[:, m, :], in_offset=None, compute_op=ALU.add).then_inc(rows_added, 16)
                    for m in range(tiles, CT):
                        pool.dma_start(spare[:, 4 + m:5 + m], fcs[0:1, m:m + 1]).then_inc(rows_added, 16)
                by_tiles(pool, n, rows)
            n_items = items(pool)
            for n in range(2):
                pool.wait_ge(xn_out[n], 16 * NT // 2)
            pool.wait_ge(zero_out, 32 * CT)
            pool.dma_start(spare[:, 9:10], fcs[0:1, 0:1]).then_inc(rows_added, 16)
            gather(0, item(pool, 1, 0))
            gather(1, item(pool, 1, 1))
            pool.wait_ge(acc_out, 16 * NT)
            with pool.Fori(0, MAX_ITEMS) as i:
                with pool.If(i < n_items):
                    n_now, n_next = item(pool, 1, i), item(pool, 1, i + 2)
                    gather(i + 2, n_next)
                    scatter(i, n_now)

        @block.scalar
        def _(act):
            act.wait_ge(consts_ready, 1)

            def norm_rms(t):
                act.wait_ge(x2_done, 2 * (t + 1))
                act.activation(junk, x2[:, t, :], ACT.Square, accum_out=ss2[:, t:t + 1])
                act.drain()
                act.activation(rms2[:, t:t + 1], ss2[:, t:t + 1], ACT.Sqrt, bias=eps_c, scale=1.0 / D).then_inc(rms2_ready, 1)

            def store_xn(t):
                act.wait_ge(xn_turned, 2 * t + 1)
                if t >= 2:
                    act.wait_ge(logits_done, t - 1)
                act.activation(xnT[t % 2][:, 0:4, :], bank[4 + 2 * (t % 2)][:, :].rearrange("p (k n) -> p k n", k=4), ACT.Copy).then_inc(xnT_act, 1)
            for t in range(NT + 4):
                if t >= 4:
                    act.wait_ge(top_ready, t - 3)
                    act.activation(ex[:, t - 4, :], top[:, t - 4, 0:TOPK], ACT.Exp, bias=ntop[:, t - 4:t - 3],
                                   accum_out=exs[:, t - 4:t - 3]).then_inc(ex_ready, 1)
                if t < NT:
                    norm_rms(t)
                if 1 <= t <= NT:
                    store_xn(t - 1)
            act.wait_ge(b1_turned, 1)
            act.activation(b1T[:, :, :].rearrange("p e f -> p f e"), bank[3][:, :].rearrange("p (f e) -> p f e", f=2 * KD), ACT.Copy).then_inc(b1_taken, 1)
            act.wait_ge(gt_done, 1)
            act.activation(gT[:, 0:512], bank[4][0:NEXP, :], ACT.Copy)
            act.activation(gT[:, 512:1024], bank[5][0:NEXP, :], ACT.Copy).then_inc(gt_taken, 1)

            def turn_x(i_next, n):

                def tiles(nt):
                    for m in range(nt):
                        act.wait_ge(x_turned, i_next * 2 * CT + (2 * m + 1))
                        act.activation(xT[:, 0:4, m * P:(m + 1) * P], bank[(6, 0, 6)[m]][:, :].rearrange("p (k n) -> p k n", k=4), ACT.Copy).then_inc(xT_act, 1 + (CT - nt) * (m == nt - 1))
                by_tiles(act, n, tiles)

            def sigmoids(i, n):

                def body(nv):
                    for f in range(KD):
                        act.wait_ge(gate_ready, i * KD + (f + 1))
                        act.activation(sg[f % 2][:, 0:nv], gl[f % 2][:, 0:nv], ACT.Sigmoid, scale=SWIGLU_ALPHA).then_inc(sig_ready, 1)
                by_slots(act, n, body)

            def store_y(i, n):

                def body(nv):
                    if nv <= P:
                        act.sem_inc(down_taken, KD)
                        return
                    for d in range(KD):
                        act.wait_ge(down_done, i * KD + (d + 1))
                        act.activation(yT[:, d, 0:nv], bank[4 + d % 2][:, 0:nv], ACT.Copy).then_inc(down_taken, 1)
                by_slots(act, n, body)

            def weigh_y(i, n):

                def tiles(nt):
                    act.wait_ge(sslots_ready, i + 1)
                    if nt == 1:
                        act.wait_ge(down_done, i * KD + KD // 2)
                        act.activation(yrow[:, 0, 0:512], bank[4][:, :], ACT.Copy, scale=gates_s[:, 0:1]).then_inc(yrow_act, CT)
                        return
                    for m in range(nt):
                        act.wait_ge(y_turned, i * 2 * CT + (2 * m + 1))
                        act.activation(yrow[:, m, 0:512], bank[(6, 4, 6)[m]][:, :], ACT.Copy, scale=gates_s[:, m:m + 1]).then_inc(yrow_act, 1 + (CT - nt) * (m == nt - 1))
                by_tiles(act, n, tiles)
            n_items = items(act)
            act.sem_inc(yrow_act, 1)
            turn_x(0, item(act, 1, 0))
            with act.Fori(0, MAX_ITEMS) as i:
                with act.If(i < n_items):
                    n_now, n_next = item(act, 1, i), item(act, 1, i + 1)
                    sigmoids(i, n_now)
                    turn_x(i + 1, n_next)
                    store_y(i, n_now)
                    weigh_y(i, n_now)
            for t in range(NT):
                act.wait_ge(f_in[t], 16)
                act.activation(fin_junk, fin[t], ACT.Square, accum_out=ss3[:, t:t + 1])
                act.drain()
                act.activation(rms3[:, t:t + 1], ss3[:, t:t + 1], ACT.Sqrt, bias=eps_c, scale=1.0 / D).then_inc(f_rms, 1)

        @block.vector
        def _(dve):
            dve.memset(eps_c, EPS).then_inc(consts_ready, 1)
            dve.memset(zero, 0.0).then_inc(consts_ready, 1)
            def residual(t):
                if t == 0:
                    dve.wait_ge(x_back, 16)
                for half in range(2):
                    v = x2[:, t, half * 512:(half + 1) * 512]
                    dve.wait_ge(o_proj, 2 * t + half + 1)
                    dve.tensor_tensor(v, v, bank[2 + half][:, :], ALU.add).then_inc(x2_done, 1)

            def norm(t):
                if t == 0:
                    dve.wait_ge(route_in, 6 * 16)
                    dve.wait_ge(order_in, 16)
                dve.wait_ge(rms2_ready, t + 1)
                dve.reciprocal(rstd2[:, t:t + 1], rms2[:, t:t + 1])
                dve.drain()
                if t >= 2:
                    dve.wait_ge(xn_turned, 2 * (t - 1))
                    dve.wait_ge(xn_out[t % 2], 16 * (t // 2))
                dve.scalar_tensor_tensor(out=xn[t % 2], in0=x2[:, t, :], scalar=rstd2[:, t:t + 1], in1=g2_b,
                                         op0=ALU.mult, op1=ALU.mult).then_inc(xn_ready, 1)

            def store_xn(t):
                dve.wait_ge(xn_turned, 2 * t + 2)
                if t >= 2:
                    dve.wait_ge(logits_done, t - 1)
                dve.tensor_copy(xnT[t % 2][:, 4:8, :], bank[5 + 2 * (t % 2)][:, :].rearrange("p (k n) -> p k n", k=4)).then_inc(xnT_dve, 1)

            def best(t):
                dve.wait_ge(logits_done, t + 1)
                dve.tensor_tensor(lg[:, t, :], bank[t % 2][:, 0:NEXP], rb_b, ALU.add).then_inc(logits_taken, 1)
                dve.drain()
                dve.max(top[:, t, :], lg[:, t, :])
                dve.drain()
                dve.max_index(topi[:, t, :], top[:, t, :], lg[:, t, :])
                dve.tensor_scalar(ntop[:, t:t + 1], top[:, t, 0:1], -1.0, None, ALU.mult)
                dve.drain()
                dve.tensor_copy(topf[:, t, :], topi[:, t, 0:TOPK]).then_inc(top_ready, 1)

            def gate(t):
                dve.wait_ge(ex_ready, t + 1)
                dve.reciprocal(rexs[:, t:t + 1], exs[:, t:t + 1])
                dve.drain()
                dve.tensor_scalar(ex[:, t, :], ex[:, t, :], rexs[:, t:t + 1], None, ALU.mult)
                for k in range(TOPK):
                    dve.tensor_scalar(hot[:, k, :], iota_e, topf[:, t, k:k + 1], None, ALU.is_equal)
                dve.drain()
                dve.tensor_tensor(maskf[:, t, :], hot[:, 0, :], hot[:, 1, :], ALU.add)
                dve.tensor_scalar(gates[:, t, :], hot[:, 0, :], ex[:, t, 0:1], None, ALU.mult)
                for k in range(1, TOPK):
                    dve.drain()
                    if k >= 2:
                        dve.tensor_tensor(maskf[:, t, :], maskf[:, t, :], hot[:, k, :], ALU.add)
                    dve.scalar_tensor_tensor(out=gates[:, t, :], in0=hot[:, k, :], scalar=ex[:, t, k:k + 1], in1=gates[:, t, :],
                                             op0=ALU.mult, op1=ALU.add)
                dve.drain()
                dve.tensor_copy(maskb[:, t, 0:NEXP], maskf[:, t, :])
                dve.tensor_copy(maskb[:, t, NEXP:CANDS], maskf[:, t, :]).then_inc(mask_ready, 1)
            for t in range(NT + 4):
                if 1 <= t <= NT:
                    norm(t - 1)
                if 2 <= t <= NT + 1:
                    store_xn(t - 2)
                if 3 <= t <= NT + 2:
                    best(t - 3)
                if t >= 4:
                    gate(t - 4)
                if t < NT:
                    residual(t)

            def add_b2(ns):
                for n in ns:
                    t, half = n // 2, n % 2
                    dve.wait_ge(b2_done, n + 1)
                    v = x2[:, t, half * 512:(half + 1) * 512]
                    dve.tensor_tensor(v, v, bank[6 + n % 2][:, :], ALU.add).then_inc(acc_ready, 1)
            gv = gates.rearrange("p t e -> p e t")
            dve.tensor_copy(gparts[:, :, :, 0], gv)
            dve.drain()
            dve.tensor_tensor(gres, gv, gparts[:, :, :, 0], ALU.subtract)
            dve.drain()
            dve.tensor_copy(gparts[:, :, :, 1], gres)
            dve.drain()
            dve.tensor_tensor(gres2, gres, gparts[:, :, :, 1], ALU.subtract)
            dve.drain()
            dve.tensor_copy(gparts[:, :, :, 2], gres2)
            dve.wait_ge(count_done, 1)
            rv = rankm[:, :, :].rearrange("p e t -> p t e")
            dve.tensor_scalar(rv, bank[2][:, 0:256].rearrange("p (t e) -> p t e", t=NT), 1.0, None, ALU.add)
            dve.drain()
            dve.tensor_tensor(rv, rv, maskf, ALU.mult)
            dve.drain()
            dve.tensor_scalar(rankm[:, :, :], rankm[:, :, :], -1.0, None, ALU.add)
            dve.memset(lists[:, :, :], 0.0)
            dve.drain()
            dve.tensor_copy(lists[:, 0, 0:NEXP], iota_e)
            dve.tensor_scalar(lists[:, 1, 0:NEXP], bank[2][:, 256:256 + NEXP], float(CAP), None, ALU.min)
            dve.tensor_copy(cand_n, bank[2][0:CANDS, 300:301])
            dve.drain()
            dve.tensor_tensor(cand_flag, cand_n, cand_first, ALU.is_gt)
            dve.tensor_scalar(cand_v[0:CANDS, 0, :], ones_f[0:CANDS, :], cand_exp, None, ALU.mult)
            dve.tensor_scalar(cand_v[0:CANDS, 2, :], ones_f[0:CANDS, :], cand_first, None, ALU.mult)
            dve.tensor_scalar(cand_n, cand_n, cand_first, float(CAP), ALU.subtract, ALU.min)
            dve.drain()
            dve.tensor_scalar(cand_v[0:CANDS, 1, :], ones_f[0:CANDS, :], cand_n, None, ALU.mult).then_inc(flag_ready, 1)
            add_b2(range(0, 2))
            dve.wait_ge(pos_done, 1)
            dve.tensor_copy(cand_pos, bank[0][0:CANDS, 0:1])
            dve.tensor_scalar(nitem[:, :], bank[0][:, 1:2], float(NEXP), None, ALU.add)
            dve.drain()
            dve.tensor_scalar(cand_hot[0:CANDS, :], iota_e[0:CANDS, 0:NLIST - NEXP], cand_pos, cand_flag, ALU.is_equal, ALU.mult).then_inc(cand_ready, 1)
            add_b2(range(2, 4))
            dve.wait_ge(list_done, 1)
            dve.tensor_copy(lists[:, :, NEXP:NLIST], bank[1][:, 0:3 * (NLIST - NEXP)].rearrange("p (v n) -> p v n", v=3))
            dve.drain()
            dve.tensor_copy(listi[:, :, :], lists[:, :, :]).then_inc(list_ready, 1)

            def slots(i_next):
                e = item(dve, 0, i_next)
                dve.tensor_copy(rk0, rankm[:, bass.ds(e, 1), :].rearrange("p o t -> p (o t)"))
                dve.tensor_copy(basec, lists[:, 2, bass.ds(i_next, 1)])
                dve.tensor_copy(gcur[:, :, 3:6], gparts[:, bass.ds(e, 1), :, :].rearrange("p o t v -> p (o t) v"))
                dve.drain()
                dve.tensor_scalar(rk, rk0, basec, None, ALU.subtract)
                dve.drain()
                for t in range(NT):
                    ins = dve.tensor_scalar(onehot[:, t, :], iota_s, rk[:, t:t + 1], None, ALU.is_equal)
                ins.then_inc(hot_ready, 1)

            def read_slots(i_next):
                dve.wait_ge(slots_done, i_next + 1)
                v = bank[5][:, 0:CT * 6].rearrange("p (m v) -> p m v", m=CT)
                dve.tensor_scalar(padf, v[:, :, 2], -1.0, 1.0, ALU.mult, ALU.add)
                dve.tensor_scalar(idxf, v[:, :, 0], float(P), None, ALU.mult)
                dve.tensor_copy(gateg, v[:, :, 3])
                dve.drain()
                dve.tensor_tensor(padf, padf, unused_row, ALU.mult)
                dve.tensor_tensor(idxf, idxf, v[:, :, 1], ALU.add)
                dve.tensor_tensor(gateg, gateg, v[:, :, 4], ALU.add)
                dve.drain()
                dve.tensor_tensor(gateg, gateg, v[:, :, 5], ALU.add)
                dve.tensor_tensor(idxf, idxf, padf, ALU.add)
                dve.drain()
                if not (isinstance(i_next, int) and i_next == 0):
                    dve.wait_ge(rows_in, 16 * CT * i_next)
                dve.tensor_copy(idxg, idxf).then_inc(slots_ready, 1)

            def turn_x(i_next, n):

                def tiles(nt):
                    for m in range(nt):
                        dve.wait_ge(x_turned, i_next * 2 * CT + (2 * m + 2))
                        dve.tensor_copy(xT[:, 4:8, m * P:(m + 1) * P], bank[(7, 1, 7)[m]][:, :].rearrange("p (k n) -> p k n", k=4)).then_inc(xT_dve, 1 + (CT - nt) * (m == nt - 1))
                by_tiles(dve, n, tiles)

            def swiglu(i, n):

                def body(nv):
                    for f in range(KD):
                        b = 2 * (f % 2)
                        g, u, s = gl[f % 2][:, 0:nv], ul[f % 2][:, 0:nv], sg[f % 2][:, 0:nv]
                        dve.wait_ge(up_done, i * KD + (f + 1))
                        dve.tensor_scalar(g, bank[b][:, 0:nv], b1c[:, f:f + 1], SWIGLU_LIMIT, ALU.add, ALU.min).then_inc(gate_ready, 1)
                        dve.tensor_scalar(u, bank[b + 1][:, 0:nv], b1c[:, KD + f:KD + f + 1], SWIGLU_LIMIT, ALU.add, ALU.min).then_inc(up_taken, 1)
                        dve.drain()
                        dve.tensor_scalar(u, u, -SWIGLU_LIMIT, 1.0, ALU.max, ALU.add)
                        dve.drain()
                        dve.wait_ge(sig_ready, i * KD + (f + 1))
                        dve.tensor_tensor(u, u, g, ALU.mult)
                        dve.drain()
                        dve.tensor_tensor(actT[:, f, 0:nv], u, s, ALU.mult).then_inc(act_ready, 1)
                by_slots(dve, n, body)

            def weigh_y(i, n):

                def tiles(nt):
                    if nt == 1:
                        dve.wait_ge(down_done, (i + 1) * KD)
                        dve.tensor_scalar(yrow[:, 0, 512:1024], bank[5][:, :], gates_s[:, 0:1], None, ALU.mult).then_inc(yrow_dve, CT)
                        return
                    for m in range(nt):
                        dve.wait_ge(y_turned, i * 2 * CT + (2 * m + 2))
                        dve.tensor_scalar(yrow[:, m, 512:1024], bank[(7, 5, 7)[m]][:, :], gates_s[:, m:m + 1], None, ALU.mult).then_inc(yrow_dve, 1 + (CT - nt) * (m == nt - 1))
                by_tiles(dve, n, tiles)

            def bias(j):
                e = item(dve, 0, j)
                dve.tensor_copy(b1c, b1T[:, bass.ds(e, 1), :].rearrange("p o f -> p (o f)"))
                dve.drain()

            def pass_on():
                dve.tensor_copy(idxa, idxg)
                dve.tensor_copy(gatea, gateg)
                dve.drain()

            def keep_slots(i):
                dve.wait_ge(rows_added, 16 * CT * i + 16)
                dve.tensor_copy(idxs, idxa)
                dve.tensor_copy(gates_s, gatea).then_inc(sslots_ready, 1)
                dve.drain()
            n_items = items(dve)
            dve.sem_inc(yrow_dve, 1)
            slots(0)
            add_b2(range(4, 6))
            read_slots(0)
            add_b2(range(6, 10))
            pass_on()
            slots(1)
            add_b2(range(10, 2 * NT))
            turn_x(0, item(dve, 1, 0))
            dve.wait_ge(zero_out, 32 * CT)
            dve.memset(yT[:, :, :], 0.0)
            dve.memset(actT[:, :, VARIANTS[0]:P], 0.0)
            read_slots(1)
            slots(2)
            dve.wait_ge(b1_taken, 1)
            bias(0)
            dve.wait_ge(acc_out, 16 * NT)
            with dve.Fori(0, MAX_ITEMS) as i:
                with dve.If(i < n_items):
                    n_now, n_next = item(dve, 1, i), item(dve, 1, i + 1)
                    swiglu(i, n_now)
                    keep_slots(i)
                    pass_on()
                    read_slots(i + 2)
                    turn_x(i + 1, n_next)
                    bias(i + 1)
                    slots(i + 3)
                    weigh_y(i, n_now)
            dve.wait_ge(f_g, 16)
            for t in range(NT):
                dve.wait_ge(f_rms, t + 1)
                dve.reciprocal(rstd3[:, t:t + 1], rms3[:, t:t + 1])
                dve.drain()
                dve.scalar_tensor_tensor(out=fin[t], in0=fin[t], scalar=rstd3[:, t:t + 1], in1=fin_g,
                                         op0=ALU.mult, op1=ALU.mult).then_inc(f_ready, 1)

        @block.tensor
        def _(pe):
            def turn_xn(t):
                pe.wait_ge(xn_ready, t + 1)
                for half in range(2):
                    if t >= 2:
                        pe.wait_ge(xnT_act if half == 0 else xnT_dve, t - 1)
                    for k in range(4):
                        ins = pe.transpose(bank[4 + 2 * (t % 2) + half][:, k * P:(k + 1) * P],
                                           xn[t % 2][:, (4 * half + k) * P:(4 * half + k + 1) * P], ident)
                    ins.then_inc(xn_turned, 1)

            def logits(t):
                if t == 0:
                    pe.wait_ge(route_in, 6 * 16)
                    pe.wait_ge(order_in, 16)
                pe.wait_ge(xnT_act, t + 1)
                pe.wait_ge(xnT_dve, t + 1)
                if t >= 2:
                    pe.wait_ge(logits_taken, t - 1)
                for k in range(KD):
                    ins = pe.matmul(bank[t % 2][:, 0:NEXP], xnT[t % 2][:, k, :], rw[:, k, :], start=(k == 0), stop=(k == KD - 1))
                ins.then_inc(logits_done, 1)
            def out_product(t):
                for half in range(2):
                    if t:
                        pe.wait_ge(x2_done, 2 * t - 1 + half)
                    for k in range(KD):
                        ins = pe.matmul(bank[2 + half][:, :], mixT[:, k, t * P:(t + 1) * P], wo_s[:, k, half * 512:(half + 1) * 512],
                                        start=(k == 0), stop=(k == KD - 1))
                    ins.then_inc(o_proj, 1)
            for t in range(NT + 2):
                if t < NT:
                    out_product(t)
                if 1 <= t <= NT:
                    turn_xn(t - 1)
                if t >= 2:
                    logits(t - 2)
            pe.wait_ge(x2_done, 2 * NT)
            for f in range(2 * KD):
                ins = pe.transpose(bank[3][:, f * NEXP:(f + 1) * NEXP], b1n[:, f * P:(f + 1) * P], ident[0:NEXP, 0:NEXP])
            ins.then_inc(b1_turned, 1)
            pe.wait_ge(mask_ready, NT)
            for t in range(NT):
                for s in range(t + 1):
                    pe.matmul(bank[2][:, t * NEXP:(t + 1) * NEXP], ones_b if s < t else tri, maskb[:, s, 0:NEXP], start=(s == 0), stop=(s == t))
            for t in range(NT):
                pe.matmul(bank[2][:, 256:256 + NEXP], ones_b, maskb[:, t, 0:NEXP], start=(t == 0), stop=(t == NT - 1))
            for t in range(NT):
                ins = pe.matmul(bank[2][0:CANDS, 300:301], maskb[:, t, :], one_b, start=(t == 0), stop=(t == NT - 1))
            ins.then_inc(count_done, 1)
            for t in range(NT):
                ins = pe.transpose(bank[4 + t // 4][0:NEXP, (t % 4) * P:(t % 4 + 1) * P], gates[:, t, :], ident)
            ins.then_inc(gt_done, 1)

            def b2_product(ns):
                for n in ns:
                    t, half = n // 2, n % 2
                    if n >= 2:
                        pe.wait_ge(acc_ready, n - 1)
                    pe.matmul(bank[6 + n % 2][:, :], gT[:, t * P:(t + 1) * P], b2n[:, half * 512:(half + 1) * 512],
                              start=True, stop=True).then_inc(b2_done, 1)
            pe.wait_ge(gt_taken, 1)
            b2_product(range(0, 2))
            pe.wait_ge(flag_ready, 1)
            pe.matmul(bank[0][0:CANDS, 0:1], cand_before, cand_flag, start=True, stop=True)
            pe.matmul(bank[0][:, 1:2], ones_f[0:CANDS, :], cand_flag, start=True, stop=True).then_inc(pos_done, 1)
            b2_product(range(2, 4))
            pe.wait_ge(cand_ready, 1)
            w = NLIST - NEXP
            for v in range(3):
                ins = pe.matmul(bank[1][:, v * w:(v + 1) * w], cand_v[0:CANDS, v, :], cand_hot[0:CANDS, :], start=True, stop=True)
            ins.then_inc(list_done, 1)

            def slots(i_next):
                pe.wait_ge(hot_ready, i_next + 1)
                for m in range(CT):
                    for t in range(NT):
                        ins = pe.matmul(bank[5][:, m * 6:(m + 1) * 6], onehot[:, t, m * P:(m + 1) * P], gcur[:, t, :],
                                        start=(t == 0), stop=(t == NT - 1))
                ins.then_inc(slots_done, 1)

            def turn_x(i_next, n):
                pe.wait_ge(rows_in, (i_next + 1) * 16 * CT)

                def tiles(nt):
                    for m in range(nt):
                        if m == 1 and not isinstance(i_next, int):
                            pe.wait_ge(up_taken, i_next * KD - 1)
                        if m == 2:
                            pe.wait_ge(xT_act, i_next * CT + 1)
                            pe.wait_ge(xT_dve, i_next * CT + 1)
                        for k in range(KD):
                            ins = pe.transpose(bank[(6, 0, 6)[m] + k // 4][:, (k % 4) * P:(k % 4 + 1) * P], xg[:, m, k * P:(k + 1) * P], ident)
                            if k % 4 == 3:
                                ins.then_inc(x_turned, 1 + 2 * (CT - nt) * (m == nt - 1 and k == KD - 1))
                by_tiles(pe, n, tiles)

            def up(i, n):
                pe.wait_ge(xT_act, (i + 1) * CT)
                pe.wait_ge(xT_dve, (i + 1) * CT)

                def body(nv):
                    for f in range(KD):
                        q, c = divmod(f * P, PC)
                        if c == 0:
                            pe.wait_ge(w1_in[q], (i + 1) * 32)
                        b = 2 * (f % 2)
                        if f >= 2:
                            pe.wait_ge(up_taken, i * KD + (f - 1))
                        for h in range(2):
                            for k in range(KD):
                                ins = pe.matmul(bank[b + h][:, 0:nv], w1r[:, q, k, h, c:c + P], xT[:, k, 0:nv], start=(k == 0), stop=(k == KD - 1))
                        ins.then_inc(up_done, 1)
                by_slots(pe, n, body)

            def down(i, n):

                def body(nv):
                    if nv <= P:
                        for q in range(PIECES):
                            pe.wait_ge(w2_in[q], (i + 1) * 16)
                            if q == 2:
                                pe.wait_ge(slots_ready, i + 3)
                            for k in range(KD):
                                if q == 0:
                                    pe.wait_ge(act_ready, i * KD + (k + 1))
                                ins = pe.matmul(bank[4 + q // 2][:, (q % 2) * PC:(q % 2 + 1) * PC], actT[:, k, 0:P], w2r[:, q, k, :],
                                                start=(k == 0), stop=(k == KD - 1))
                            ins.then_inc(down_done, KD // PIECES)
                        return
                    for d in range(KD):
                        q, c = divmod(d * P, PC)
                        if c == 0:
                            pe.wait_ge(w2_in[q], (i + 1) * 16)
                        if d >= 2:
                            pe.wait_ge(down_taken, i * KD + (d - 1))
                        if d == 1:
                            pe.wait_ge(slots_ready, i + 3)
                        for k in range(KD):
                            if d == 0:
                                pe.wait_ge(act_ready, i * KD + (k + 1))
                            ins = pe.matmul(bank[4 + d % 2][:, 0:nv], w2r[:, q, k, c:c + P], actT[:, k, 0:nv], start=(k == 0), stop=(k == KD - 1))
                        ins.then_inc(down_done, 1)
                by_slots(pe, n, body)

            def turn_y(i, n):

                def tiles(nt):
                    if nt == 1:
                        pe.sem_inc(y_turned, 2 * CT)
                        return
                    pe.wait_ge(down_taken, (i + 1) * KD)
                    pe.wait_ge(xT_act, (i + 2) * CT)
                    pe.wait_ge(xT_dve, (i + 2) * CT)
                    for m in range(nt):
                        if m == 2:
                            pe.wait_ge(yrow_act, i * CT + 2)
                            pe.wait_ge(yrow_dve, i * CT + 2)
                        for k in range(KD):
                            ins = pe.transpose(bank[(6, 4, 6)[m] + k // 4][:, (k % 4) * P:(k % 4 + 1) * P], yT[:, k, m * P:(m + 1) * P], ident)
                            if k % 4 == 3:
                                ins.then_inc(y_turned, 1 + 2 * (CT - nt) * (m == nt - 1 and k == KD - 1))
                by_tiles(pe, n, tiles)
            n_items = items(pe)
            b2_product(range(4, 6))
            slots(0)
            b2_product(range(6, 2 * NT))
            pe.wait_ge(slots_ready, 1)
            slots(1)
            pe.wait_ge(acc_ready, 2 * NT)
            turn_x(0, item(pe, 1, 0))
            reg_now, reg_next, reg_after = (pe.alloc_register(n) for n in ("tokens_now", "tokens_next", "tokens_after"))
            pe.reg_load(reg_now, listi[0:1, 1, 0:1])
            pe.reg_load(reg_next, listi[0:1, 1, 1:2])
            with pe.Fori(0, MAX_ITEMS) as i:
                with pe.If(i < n_items):
                    n_now, n_next = pe.snap(reg_now), pe.snap(reg_next)
                    up(i, n_now)
                    pe.reg_load(reg_after, listi[0:1, 1, bass.ds(i + 2, 1)])
                    pe.wait_ge(yrow_act, i * CT + 1)
                    pe.wait_ge(yrow_dve, i * CT + 1)
                    slots(i + 2)
                    turn_x(i + 1, n_next)
                    down(i, n_now)
                    turn_y(i, n_now)
                    pe.reg_mov(reg_now, reg_next)
                    pe.reg_mov(reg_next, reg_after)


_INS = ["x", "attn_norm_g", "w_in", "b_in", "swa_sinks", "diff_lambda_q1", "diff_lambda_k1", "diff_lambda_q2", "diff_lambda_k2",
        "diff_subln_g", "w_swa_out", "w_diff_out", "w_o", "ffn_norm_g", "router_w", "router_b", "w1", "b1", "w2", "b2", "final_norm_g"]


def kernel(**inputs):
    import concourse.bacc as bacc
    from concourse.bass_utils import run_bass_kernel_spmd

    nc = bacc.Bacc("TRN2", target_bir_lowering=False, num_devices=1)
    arrays, args = {}, {}
    for name in _INS:
        v = np.ascontiguousarray(inputs[name])
        arrays[f"in_{name}"] = v
        args[name] = nc.dram_tensor(f"in_{name}", v.shape, mybir.dt.from_np(v.dtype), kind="ExternalInput").ap()
    args["out"] = nc.dram_tensor("out_rows", (1, S, D), F32, kind="ExternalOutput").ap()
    program(nc, args)
    r = run_bass_kernel_spmd(nc, [arrays], core_ids=[0])
    return r.results[0]["out_rows"]
```
